# Optimizing a Trainium2 kernel written in Bass

```python
import math
import jax, jax.numpy as jnp
from jax import lax
import numpy as np

D_MODEL = 1024
BATCH = 1
SEQ = 1024
DEPTH = 2

CHUNK = 64
N_META = 16
N_A_LAYERS = DEPTH // 2
N_B_LAYERS = DEPTH - N_A_LAYERS
GDN_HEADS = 8
GDN_HEAD_DIM = 128
GDN_WIDTH = GDN_HEADS * GDN_HEAD_DIM
CONV_WIDTH = 4
SB_HEADS = 16
SB_HEAD_DIM = 64
SB_WIDTH = SB_HEADS * SB_HEAD_DIM
SB_BLOCK = 128
D_FF = -(-(8 * D_MODEL) // (3 * 256)) * 256
GDN_IN_COLS = 4 * GDN_WIDTH + 2 * GDN_HEADS
EPS = 1e-6

kernel_name = "yoco_gdn_stickbreaking_hybrid"

def rms_norm(x, g):
    xf = x.astype(jnp.float32)
    y = xf * lax.rsqrt(jnp.mean(xf * xf, axis=-1, keepdims=True) + EPS)
    return (y * g.astype(jnp.float32)).astype(x.dtype)

def l2_normalize(x):
    return x * lax.rsqrt(jnp.sum(x * x, axis=-1, keepdims=True) + EPS)

def causal_depthwise_conv(x, w):
    L = x.shape[1]
    xp = jnp.pad(x, ((0, 0), (CONV_WIDTH - 1, 0), (0, 0)))
    return sum(xp[:, i:i + L] * w[i] for i in range(CONV_WIDTH))

def gated_delta_chunked(q, k, v, g, beta):
    b, nh, L, dk = q.shape
    dv = v.shape[-1]
    n = L // CHUNK
    q = q.reshape(b, nh, n, CHUNK, dk) * (dk ** -0.5)
    k = k.reshape(b, nh, n, CHUNK, dk)
    v = v.reshape(b, nh, n, CHUNK, dv)
    g = g.reshape(b, nh, n, CHUNK)
    beta = beta.reshape(b, nh, n, CHUNK)
    G = jnp.cumsum(g, axis=-1)
    incl = jnp.tril(jnp.ones((CHUNK, CHUNK), dtype=bool))
    strict = jnp.tril(jnp.ones((CHUNK, CHUNK), dtype=bool), -1)
    diff = G[..., :, None] - G[..., None, :]
    decay = jnp.where(incl, jnp.exp(jnp.where(incl, diff, 0.0)), 0.0)
    kk = jnp.einsum('bhnid,bhnjd->bhnij', k, k)
    lower = jnp.eye(CHUNK, dtype=q.dtype) + jnp.where(strict, beta[..., :, None] * decay * kk, 0.0)
    rhs = jnp.concatenate([beta[..., None] * v, (beta * jnp.exp(G))[..., None] * k], axis=-1)
    sol = lax.linalg.triangular_solve(lower, rhs, left_side=True, lower=True, unit_diagonal=True)
    u_base = sol[..., :dv]
    w_corr = sol[..., dv:]
    attn = jnp.einsum('bhnid,bhnjd->bhnij', q, k) * decay
    q_dec = q * jnp.exp(G)[..., None]
    g_last = G[..., -1]
    k_dec = k * jnp.exp(g_last[..., None] - G)[..., None]

    def step(S, inp):
        u_b, w_c, a_c, qd, kd, gl = inp
        u = u_b - jnp.einsum('bhcd,bhde->bhce', w_c, S)
        o = jnp.einsum('bhcd,bhde->bhce', qd, S) + jnp.einsum('bhij,bhje->bhie', a_c, u)
        S = S * jnp.exp(gl)[..., None, None] + jnp.einsum('bhcd,bhce->bhde', kd, u)
        return S, o

    xs = tuple(jnp.moveaxis(t, 2, 0) for t in (u_base, w_corr, attn, q_dec, k_dec, g_last))
    S0 = jnp.zeros((b, nh, dk, dv), dtype=q.dtype)
    _, o = lax.scan(step, S0, xs)
    return jnp.moveaxis(o, 0, 2).reshape(b, nh, L, dv)

def gdn_mixer(h, w_in, conv_w, a_log, dt_bias, onorm_g, w_out):
    b, L, _ = h.shape
    proj = h @ w_in
    qkv = jax.nn.silu(causal_depthwise_conv(proj[..., :3 * GDN_WIDTH], conv_w)).astype(jnp.float32)
    gate = proj[..., 3 * GDN_WIDTH:4 * GDN_WIDTH].astype(jnp.float32)
    a_in = proj[..., 4 * GDN_WIDTH:4 * GDN_WIDTH + GDN_HEADS].astype(jnp.float32)
    b_in = proj[..., 4 * GDN_WIDTH + GDN_HEADS:].astype(jnp.float32)
    heads = lambda t: t.reshape(b, L, GDN_HEADS, GDN_HEAD_DIM).transpose(0, 2, 1, 3)
    q = l2_normalize(heads(qkv[..., :GDN_WIDTH]))
    k = l2_normalize(heads(qkv[..., GDN_WIDTH:2 * GDN_WIDTH]))
    v = heads(qkv[..., 2 * GDN_WIDTH:])
    g = (-jnp.exp(a_log.astype(jnp.float32)) * jax.nn.softplus(a_in + dt_bias.astype(jnp.float32))).transpose(0, 2, 1)
    beta = jax.nn.sigmoid(b_in).transpose(0, 2, 1)
    front = (-N_META) % CHUNK
    back = (-(front + L)) % CHUNK
    p4 = ((0, 0), (0, 0), (front, back), (0, 0))
    p3 = ((0, 0), (0, 0), (front, back))
    o = gated_delta_chunked(jnp.pad(q, p4), jnp.pad(k, p4), jnp.pad(v, p4), jnp.pad(g, p3), jnp.pad(beta, p3))
    o = o[:, :, front:front + L].transpose(0, 2, 1, 3)
    o = o * lax.rsqrt(jnp.mean(o * o, axis=-1, keepdims=True) + EPS) * onorm_g.astype(jnp.float32)
    o = o * jax.nn.silu(gate.reshape(b, L, GDN_HEADS, GDN_HEAD_DIM))
    return o.reshape(b, L, GDN_WIDTH).astype(h.dtype) @ w_out

def shared_kv(h, norm_g, w_kv):
    b, L, _ = h.shape
    kv = (rms_norm(h, norm_g) @ w_kv).astype(jnp.float32).reshape(b, L, 2, SB_HEADS, SB_HEAD_DIM)
    return kv[:, :, 0].transpose(0, 2, 1, 3), kv[:, :, 1].transpose(0, 2, 1, 3)

def sb_mixer(h, k_sh, v_sh, w_q, w_o):
    b, L, _ = h.shape
    q = (h @ w_q).astype(jnp.float32).reshape(b, L, SB_HEADS, SB_HEAD_DIM).transpose(0, 2, 1, 3)
    pad = (-L) % SB_BLOCK
    Lp = L + pad
    p4 = ((0, 0), (0, 0), (0, pad), (0, 0))
    q, k, v = jnp.pad(q, p4), jnp.pad(k_sh, p4), jnp.pad(v_sh, p4)
    nb = Lp // SB_BLOCK
    q_blocks = q.reshape(b, SB_HEADS, nb, SB_BLOCK, SB_HEAD_DIM).transpose(2, 0, 1, 3, 4)
    key_pos = jnp.arange(Lp)
    scale = SB_HEAD_DIM ** -0.5

    def one_block(args):
        q_blk, blk = args
        q_pos = blk * SB_BLOCK + jnp.arange(SB_BLOCK)
        visible = key_pos[None, :] < q_pos[:, None]
        z = jnp.einsum('bhqd,bhkd->bhqk', q_blk, k) * scale
        log_beta = jax.nn.log_sigmoid(z)
        log_keep = jnp.where(visible, log_beta - z, 0.0)
        log_w = log_beta + lax.cumsum(log_keep, axis=3, reverse=True) - log_keep
        w = jnp.where(visible, jnp.exp(log_w), 0.0)
        return jnp.einsum('bhqk,bhkd->bhqd', w, v)

    o = lax.map(one_block, (q_blocks, jnp.arange(nb)))
    o = o.transpose(1, 2, 0, 3, 4).reshape(b, SB_HEADS, Lp, SB_HEAD_DIM)[:, :, :L]
    o = o.transpose(0, 2, 1, 3).reshape(b, L, SB_WIDTH).astype(h.dtype)
    return o @ w_o

def swiglu(h, w_gate_up, w_down):
    gu = h @ w_gate_up
    return (jax.nn.silu(gu[..., :D_FF]) * gu[..., D_FF:]) @ w_down

def setup_inputs(seed: int = 0) -> dict:
    key = jax.random.key(seed)
    ks = jax.random.split(key, 20)
    f32 = jnp.float32
    dense = lambda k, shape, fan_in: jax.random.normal(k, shape, f32) * (fan_in ** -0.5)
    gain = lambda k, shape: 1.0 + 0.02 * jax.random.normal(k, shape, f32)
    dt = jnp.exp(jax.random.uniform(ks[5], (N_A_LAYERS, GDN_HEADS), f32, math.log(1e-3), math.log(1e-1)))
    return {
        "x": jax.random.normal(ks[0], (BATCH, SEQ, D_MODEL), f32),
        "meta_tokens": jax.random.normal(ks[1], (N_META, D_MODEL), f32),
        "gdn_norm_g": gain(ks[2], (N_A_LAYERS, D_MODEL)),
        "gdn_w_in": dense(ks[3], (N_A_LAYERS, D_MODEL, GDN_IN_COLS), D_MODEL),
        "gdn_conv_w": dense(ks[4], (N_A_LAYERS, CONV_WIDTH, 3 * GDN_WIDTH), CONV_WIDTH),
        "gdn_a_log": jnp.log(jax.random.uniform(ks[6], (N_A_LAYERS, GDN_HEADS), f32, 1.0, 16.0)),
        "gdn_dt_bias": dt + jnp.log(-jnp.expm1(-dt)),
        "gdn_onorm_g": gain(ks[7], (N_A_LAYERS, GDN_HEAD_DIM)),
        "gdn_w_out": dense(ks[8], (N_A_LAYERS, GDN_WIDTH, D_MODEL), GDN_WIDTH),
        "kv_norm_g": gain(ks[9], (D_MODEL,)),
        "w_kv": dense(ks[10], (D_MODEL, 2 * SB_WIDTH), D_MODEL),
        "sb_norm_g": gain(ks[11], (N_B_LAYERS, D_MODEL)),
        "sb_w_q": dense(ks[12], (N_B_LAYERS, D_MODEL, SB_WIDTH), D_MODEL),
        "sb_w_o": dense(ks[13], (N_B_LAYERS, SB_WIDTH, D_MODEL), SB_WIDTH),
        "ffn_norm_g": gain(ks[14], (DEPTH, D_MODEL)),
        "ffn_w_gate_up": dense(ks[15], (DEPTH, D_MODEL, 2 * D_FF), D_MODEL),
        "ffn_w_down": dense(ks[16], (DEPTH, D_FF, D_MODEL), D_FF),
        "final_norm_g": gain(ks[17], (D_MODEL,)),
    }

def reference(x, meta_tokens, gdn_norm_g, gdn_w_in, gdn_conv_w, gdn_a_log, gdn_dt_bias,
              gdn_onorm_g, gdn_w_out, kv_norm_g, w_kv, sb_norm_g, sb_w_q, sb_w_o,
              ffn_norm_g, ffn_w_gate_up, ffn_w_down, final_norm_g):
    b = x.shape[0]
    meta = jnp.broadcast_to(meta_tokens.astype(x.dtype)[None], (b, N_META, D_MODEL))
    h = jnp.concatenate([meta, x], axis=1)
    k_sh = None
    v_sh = None
    for layer in range(DEPTH):
        if layer < N_A_LAYERS:
            h = h + gdn_mixer(rms_norm(h, gdn_norm_g[layer]), gdn_w_in[layer], gdn_conv_w[layer],
                              gdn_a_log[layer], gdn_dt_bias[layer], gdn_onorm_g[layer], gdn_w_out[layer])
        else:
            j = layer - N_A_LAYERS
            h = h + sb_mixer(rms_norm(h, sb_norm_g[j]), k_sh, v_sh, sb_w_q[j], sb_w_o[j])
        h = h + swiglu(rms_norm(h, ffn_norm_g[layer]), ffn_w_gate_up[layer], ffn_w_down[layer])
        if layer == N_A_LAYERS - 1:
            k_sh, v_sh = shared_kv(h, kv_norm_g, w_kv)
    return rms_norm(h, final_norm_g)[:, N_META:]


_drawn_inputs = setup_inputs


def setup_inputs(seed=0):
    import zlib

    import numpy as np

    out = dict(_drawn_inputs(seed))
    spreads = {}
    factors = {'gdn_onorm_g': 4.438,
     'kv_norm_g': 5.395,
     'sb_norm_g': 8.0,
     'ffn_norm_g': 3.021,
     'final_norm_g': 2.872}
    for name, (base, spread) in spreads.items():
        noise = np.random.default_rng([zlib.crc32(name.encode()), seed]).standard_normal(out[name].shape)
        drawn = base * np.exp(spread * noise) if base else spread * noise
        out[name] = __import__('jax').numpy.asarray(drawn.astype(out[name].dtype))
    for name, factor in factors.items():
        out[name] = (out[name] * factor).astype(out[name].dtype)
    return out
```

```python
import concourse.bass as bass
from concourse import mybir
from contextlib import ExitStack

F32 = mybir.dt.float32
F32R = mybir.dt.float32r
BF16 = mybir.dt.bfloat16
ALU = mybir.AluOpType
ACT = mybir.ActivationFunctionType

D = 1024
KT = D // 128
SEQ = 1024
META = 16
L = SEQ + META
GH, GD = 8, 128
FF = 2816
EPS = 1e-6
C = 104
NC = L // C
HG = 4
GW = HG * C
LEVELS = 7
LTB = 3
NEG = -1e30
QB = SEQ // 128
PAIRS = 8
ALL_CH = [(0, 348), (348, 346), (694, 346)]
SEQ_CH = [(META, 512), (META + 512, 512)]
SEQ_NCH = [(META + 256 * i, 256) for i in range(4)]
FG = FF // 256


class Phase:

    def __init__(self, jobs, ring, chunks, prev, mm_jobs=None):
        self.jobs, self.ring, self.chunks, self.nch = jobs, ring, chunks, len(chunks)
        self.job0 = prev.job0 + prev.jobs if prev else 0
        self.mm0 = prev.mm0 + prev.mm if prev else 0
        self.mm = (jobs if mm_jobs is None else mm_jobs) * self.nch
        self.slot0 = [prev.slot0[s] + prev.used(s) for s in range(6)] if prev else [0] * 6

    def used(self, s):
        return len(range(s, self.jobs, self.ring)) if s < self.ring else 0


P_IN = Phase(32, 4, ALL_CH, None)
P_GO = Phase(8, 4, ALL_CH, P_IN)
P_F0 = Phase(6 * FG, 6, ALL_CH, P_GO, 4 * FG)
P_KV = Phase(16, 4, ALL_CH, P_F0)
P_Q = Phase(8, 4, SEQ_CH, P_KV)
P_O = Phase(8, 4, SEQ_CH, P_Q)
P_F1 = Phase(6 * FG, 6, SEQ_CH, P_O, 4 * FG)

TAKEN0 = {P_IN: 0, P_GO: 96, P_KV: 120, P_Q: 168, P_O: 184}
SMALL = 16


def level_blocks(b):
    full = C // (2 * b)
    rest = C - full * 2 * b
    return ([(0, full, 2 * b)] if full else []) + ([(full * 2 * b, 1, rest)] if rest else [])


CONSTS = 5 + sum(3 if w > 1 << v else 1 for v in range(LEVELS) for _, _, w in level_blocks(1 << v))


def tr_groups(i):
    return [(0, min(4, i + 1))] + ([(4, i - 3)] if i > 3 else []) + [(8, 1)]


def tr_before(u):
    return sum(len(tr_groups(v // 2)) for v in range(u))


TRG = tr_before(2 * QB)


def down_banks(nch):
    return list(range(2 * nch, 8)) + list(range(nch, 2 * nch))


def trunk(nc, x, meta_tokens, gdn_norm_g, gdn_w_in, gdn_conv_w, gdn_a_log, gdn_dt_bias, gdn_onorm_g,
          gdn_w_out, kv_norm_g, w_kv, sb_norm_g, sb_w_q, sb_w_o, ffn_norm_g, ffn_w_gate_up,
          ffn_w_down, final_norm_g, out):
    ds = bass.ds
    s_in = nc.dram_tensor("s_in", (NC, 128, 32 * C), F32).ap()
    s_kv = nc.dram_tensor("s_kv", (16, 128, L), F32).ap()
    s_q = nc.dram_tensor("s_q", (8, 128, SEQ), F32).ap()
    s_in_w = s_in.rearrange("c p (t j) -> t p c j", t=32)
    w_in = gdn_w_in[0].rearrange("(k p) n -> p k n", p=128)
    w_go = gdn_w_out[0].rearrange("(k p) n -> p k n", p=128)
    w_kvv = w_kv.rearrange("(k p) n -> p k n", p=128)
    w_q = sb_w_q[0].rearrange("(k p) n -> p k n", p=128)
    w_o = sb_w_o[0].rearrange("(k p) n -> p k n", p=128)
    w_gu = [ffn_w_gate_up[i].rearrange("(k p) n -> p k n", p=128) for i in range(2)]
    w_dn = [ffn_w_down[i].rearrange("(t p) n -> t p n", p=128) for i in range(2)]

    ctx = ExitStack()
    with ctx:
        def sem(name):
            return ctx.enter_context(nc.semaphore(name))

        def keep(name, shape, dt=F32):
            return ctx.enter_context(nc.sbuf_tensor(name, shape, dt))

        hT = keep("hT", [128, KT, L])
        XH = keep("XH", [128, KT, L], F32R)
        XL = keep("XL", [128, KT, L], F32R)
        ident = keep("ident", [128, 128])
        ones = keep("ones", [128, 128])
        tri = keep("tri", [C, C])
        negm = keep("negm", [C, C])
        lvl = keep("lvl", [C, LEVELS, C])
        identb = keep("identb", [128, 128], BF16)
        maskb = keep("maskb", [128, 128], BF16)
        pvec = keep("pvec", [128, 121 + 24])
        epsc = keep("epsc", [128, 4])
        ab = keep("ab", [C, NC, 16])
        sm = keep("sm", [C, NC, 40])
        wab = keep("wab", [128, KT, 16])
        wabH = keep("wabH", [128, KT, 16], F32R)
        wabL = keep("wabL", [128, KT, 16], F32R)
        CONV, GN, ON, KVN, SBN, FN, FIN = 0, 96, 104, 105, 113, 121, 137

        with ExitStack() as a:
            def dense(name, shape, dt=F32):
                return a.enter_context(nc.sbuf_tensor(name, shape, dt))
            raw = [dense(f"raw{s}", [128, D]) for s in range(6)]
            WH = [dense(f"WH{s}", [128, D], F32R) for s in range(6)]
            WL = [dense(f"WL{s}", [128, D], F32R) for s in range(6)]
            rs = dense("rs", [128, 2, 348])
            with ExitStack() as b:
                sqb = b.enter_context(nc.sbuf_tensor("sqb", [128, KT, 348], F32))
                xnb = b.enter_context(nc.sbuf_tensor("xnb", [128, KT, 348], F32))
            with ExitStack() as b:
                cin = b.enter_context(nc.sbuf_tensor("cin", [128, L + 3], F32))
                cac = b.enter_context(nc.sbuf_tensor("cac", [128, L], F32))
                obuf = b.enter_context(nc.sbuf_tensor("obuf", [128, 2, L], F32))
            with ExitStack() as b:
                gact = b.enter_context(nc.sbuf_tensor("gact", [128, L], F32))
                aact = b.enter_context(nc.sbuf_tensor("aact", [128, L], F32))
                AH = b.enter_context(nc.sbuf_tensor("AH", [128, 2, L], F32R))
                AL = b.enter_context(nc.sbuf_tensor("AL", [128, 2, L], F32R))
        with ExitStack() as a:
            prow = a.enter_context(nc.sbuf_tensor("prow", [128, 128], F32))
            prow2 = a.enter_context(nc.sbuf_tensor("prow2", [24, 128], F32))
            xin = a.enter_context(nc.sbuf_tensor("xin", [128, 9, D], F32))
        with ExitStack() as a:
            def core(name, shape, dt=F32):
                return a.enter_context(nc.sbuf_tensor(name, shape, dt))
            Xc = core("Xc", [128, 24, C])
            Gt = core("Gt", [128, 8, C])
            cur = core("cur", [C, 40])
            alog = core("alog", [C, 8])
            dtb = core("dtb", [C, 8])
            t80 = [core(f"t80_{i}", [C, NC, 8]) for i in range(4)]
            B = [{n: core(f"{n}{g}", s) for n, s in [
                ("sq", [128, 2, GW]), ("rr", [128, 2, GW]), ("EG", [128, GW]),
                ("KQ", [128, 2, GW]), ("dec", [128, GW]), ("Qd", [128, GW]), ("NT", [C, GW]),
                ("attn", [C, GW]), ("LT", [C, LTB, GW]), ("U", [C, GW]), ("T", [C, GW]),
                ("X", [C, GW]), ("V", [C, 512]), ("K", [C, 512]), ("Kd", [C, 512]),
                ("Ke", [C, 512]), ("u", [C, 512]), ("S", [128, 512]),
                ("o", [128, GW]), ("kdx", [C, HG])]} for g in range(2)]
            for b in B:
                b["tg"], b["WT"], b["on"] = b["X"], b["dec"], b["Qd"]
        with ExitStack() as a:
            def att(name, shape, dt=F32):
                return a.enter_context(nc.sbuf_tensor(name, shape, dt))
            kq = [att(f"kq{i}", [128, L + SEQ]) for i in range(2)]
            vT = [att(f"vT{i}", [128, L]) for i in range(2)]
            Vt = att("Vt", [128, 9, 128])
            kp = [att(f"kp{i}", [128, L]) for i in range(2)]
            sg = [att(f"sg{i}", [128, L]) for i in range(2)]
            Pr = [att(f"Pr{i}", [128, L + 1]) for i in range(2)]
            wt = [att(f"wt{i}", [128, L]) for i in range(2)]
            wT = [att(f"wT{i}", [128, 9, 128]) for i in range(2)]
        with ExitStack() as a:
            fo = a.enter_context(nc.sbuf_tensor("fo", [128, 2, D], F32))
        PS = ctx.enter_context(nc.psum_tensor("PS", [128, 8, 512], F32))

        raw_in = [sem(f"raw_in{s}") for s in range(6)]
        w_hi = sem("w_hi")
        w_lo = sem("w_lo")
        mm_chunk = sem("mm_chunk")
        taken = sem("taken")
        d_mm = sem("d_mm")
        d_add = sem("d_add")
        sq_r, ss_r, r_r, xn_r, xh_r, xl_r = (sem(n) for n in (
            "sq_r", "ss_r", "r_r", "xn_r", "xh_r", "xl_r"))
        ssln, cin0, c_dt = sem("ssln"), sem("cin0"), sem("c_dt")
        x_in, p_in, cst, cst2, x_tr, x_cpa, x_cpv, p_tr, p_cp = (sem(n) for n in (
            "x_in", "p_in", "cst", "cst2", "x_tr", "x_cpa", "x_cpv", "p_tr", "p_cp"))
        ab_in, ab_h, ab_l, ab_mm, ab_cp, sml = (sem(n) for n in (
            "ab_in", "ab_h", "ab_l", "ab_mm", "ab_cp", "sml"))
        conv = sem("conv")
        ob = sem("ob")
        stored = [sem("stored0"), sem("stored1")]
        silu_g, act_a, act_h, act_l = (sem(n) for n in ("silu_g", "act_a", "act_h", "act_l"))
        o_tr, o_cpa, o_cpv, o_out = sem("o_tr"), sem("o_cpa"), sem("o_cpv"), [sem("o_out0"), sem("o_out1")]

        block = ctx.enter_context(nc.Block())

        NORMS, n0 = {}, 0
        for name, chs, col in (("gdn", ALL_CH, GN), ("f0", ALL_CH, FN), ("kv", ALL_CH, KVN),
                               ("sb", SEQ_NCH, SBN), ("f1", SEQ_NCH, FN + 8), ("fin", SEQ_NCH, FIN)):
            NORMS[name] = (chs, n0, col)
            n0 += len(chs)
        XL0 = {n: NORMS[n][1] for n in NORMS}

        def xn_needed(norm, ph, ch):
            return XL0[norm] + (ch + 1) * (len(NORMS[norm][0]) // ph.nch)

        cs = {}
        for n in ("sq tg ss gb rn eg kn dm qd dmm dec kk tr att nt0 vt kt kde nt lt u1 t1p t1 x xc tu t u "
                  "wt wtc up us op sp sm2 snew oc osq oss orn on1 on2 oh ol").split():
            cs[n] = [sem(f"c_{n}{g}") for g in range(2)]
        c_load, c_gate, c_cur, c_s0 = sem("c_load"), sem("c_gate"), sem("c_cur"), sem("c_s0")
        t_load = [sem("t_load0"), sem("t_load1")]
        t_vt, t_vc, t_z, t_kp, t_sg, t_p, t_w, t_tr, t_tc, t_o, t_oh, t_ol, t_one = (
            sem(f"t_{n}") for n in "vt vc z kp sg p w tr tc o oh ol one".split())

        def weights_of(ph, j, layer=0):
            w = {P_GO: w_go, P_KV: w_kvv, P_Q: w_q, P_O: w_o}[ph]
            return w[:, :, ds(j * 128, 128)]

        def slot3(t):
            return t[:, :].rearrange("p (k n) -> p k n", k=KT)

        def ffn_jobs(layer, g, last=False):
            gu, dn = w_gu[layer], w_dn[layer]
            col = g * 256
            return [gu[:, :, ds(FF + col, 128)], gu[:, :, ds(col + 128, 128)],
                    gu[:, :, ds(FF + col + 128, 128)],
                    None if last else gu[:, :, ds(col + 256, 128)], (dn, g * 2), (dn, g * 2 + 1)]

        @block.sync
        def _(sp):
            sp.dma_start(prow[0:96, :], gdn_conv_w[0].rearrange("w (t p) -> (w t) p", p=128)).then_inc(p_in, 16)
            for col, v in ((GN, gdn_norm_g[0]), (KVN, kv_norm_g), (SBN, sb_norm_g[0])):
                sp.dma_start(prow[col:col + 8, :], v.rearrange("(t p) -> t p", p=128)).then_inc(p_in, 16)
            sp.dma_start(prow[ON:ON + 1, :], gdn_onorm_g).then_inc(p_in, 16)
            sp.dma_start(prow2[0:16, :], ffn_norm_g.rearrange("l (t p) -> (l t) p", p=128)).then_inc(p_in, 16)
            sp.dma_start(prow2[16:24, :], final_norm_g.rearrange("(t p) -> t p", p=128)).then_inc(p_in, 16)
            sp.dma_start(xin[0:META, 8, :], meta_tokens).then_inc(x_in, 16)
            sp.dma_start(xin[:, 0:8, :], x[0].rearrange("(t p) n -> p t n", p=128)).then_inc(x_in, 16)
            sp.wait_ge(x_cpa, 9)
            sp.wait_ge(x_cpv, 9)
            sp.wait_ge(p_cp, 2)
            sp.dma_start(wab[:, :, :], w_in[:, :, 4 * D:4 * D + 16]).then_inc(ab_in, 16)
            for s in range(4):
                sp.dma_start(slot3(raw[s]), w_in[:, :, s * D:s * D + 128]).then_inc(raw_in[s], 16)
            with sp.Fori(0, GH - 1) as h:
                for s in range(4):
                    sp.wait_ge(w_lo, h * 4 + s + 1)
                    sp.dma_start(slot3(raw[s]), w_in[:, :, ds(h * 128 + s * D + 128, 128)]).then_inc(raw_in[s], 16)
            for b in range(2):
                sp.wait_ge(stored[b], 16 * 16)
            sp.wait_ge(mm_chunk, P_GO.mm0)
            sp.dma_start(alog[:, :], gdn_a_log[0:1, :].broadcast_to([C, 8])).then_inc(c_dt, 16)
            sp.dma_start(dtb[:, :], gdn_dt_bias[0:1, :].broadcast_to([C, 8])).then_inc(c_dt, 16)
            with sp.Fori(0, NC) as c:
                for g in range(2):
                    sp.wait_ge(cs["kn"][g], c)
                    sp.wait_ge(cs["sq"][g], c)
                    sp.wait_ge(cs["tr"][g], c)
                sp.dma_start(Xc[:, :, :], s_in[ds(c, 1), :, 0:24 * C].rearrange("a p (t j) -> p (a t) j", j=C)).then_inc(c_load, 16)
                for g in range(2):
                    sp.wait_ge(cs["on2"][g], c)
                sp.dma_start(Gt[:, :, :], s_in[ds(c, 1), :, 24 * C:32 * C].rearrange("a p (t j) -> p (a t) j", j=C)).then_inc(c_gate, 16)
            for g in range(2):
                sp.wait_ge(cs["ol"][g], NC)
                sp.wait_ge(cs["snew"][g], NC)

            def plain(ph):
                for l in range(ph.jobs):
                    if l < ph.ring:
                        sp.wait_ge(w_lo, ph.job0)
                    else:
                        sp.wait_ge(w_lo, ph.job0 + l - ph.ring + 1)
                    sp.dma_start(slot3(raw[l % 4]), weights_of(ph, l)).then_inc(raw_in[l % 4], 16)

            def ffn(ph, layer):
                sp.wait_ge(w_lo, ph.job0)
                sp.dma_start(slot3(raw[0]), w_gu[layer][:, :, 0:128]).then_inc(raw_in[0], 16)

                def group(g, first, last):
                    for i, src in enumerate(ffn_jobs(layer, g, last)):
                        if src is None:
                            continue
                        s = (1 + i - (last and i > 3)) % 6
                        if not (first and s):
                            sp.wait_ge(w_lo, g * 6 + (ph.job0 + 1 + i - (last and i > 3) - 5))
                        dst = raw[s]
                        if isinstance(src, tuple):
                            sp.dma_start(dst[:, :], src[0][ds(src[1], 1)].rearrange("a p n -> p (a n)")).then_inc(raw_in[s], 16)
                        else:
                            sp.dma_start(slot3(dst), src).then_inc(raw_in[s], 16)
                group(0, True, False)
                with sp.Fori(1, FG - 1) as g:
                    group(g, False, False)
                group(FG - 1, False, True)

            plain(P_GO)
            ffn(P_F0, 0)
            plain(P_KV)
            plain(P_Q)
            sp.wait_ge(mm_chunk, P_O.mm0)
            for b in range(2):
                sp.wait_ge(stored[b], 16 * 28)

            def pair(j, b):
                sp.dma_start(kq[b][:, 0:L], s_kv[ds(j, 1)].rearrange("a p n -> p (a n)")).then_inc(t_load[b], 16)
                sp.dma_start(kq[b][:, L:L + SEQ], s_q[ds(j, 1)].rearrange("a p n -> p (a n)")).then_inc(t_load[b], 16)
                sp.dma_start(vT[b][:, :], s_kv[ds(j + 8, 1)].rearrange("a p n -> p (a n)")).then_inc(t_load[b], 16)
            pair(0, 0)
            pair(1, 1)
            with sp.Fori(0, PAIRS // 2 - 1) as i:
                for b in range(2):
                    sp.wait_ge(t_z, i * 32 + 16 * (b + 1))
                    pair(i * 2 + 2 + b, b)
            sp.wait_ge(t_ol, QB * PAIRS)
            plain(P_O)
            ffn(P_F1, 1)
            for t in range(QB):
                sp.wait_ge(o_cpa, t + 1)
                sp.wait_ge(o_cpv, t + 1)
                sp.dma_start(out[0, t * 128:(t + 1) * 128, :], fo[:, t % 2, :]).then_inc(o_out[t % 2], 16)
            for b in range(2):
                sp.wait_ge(o_out[b], 16 * QB // 2)
            for b in range(2):
                sp.wait_ge(stored[b], 16 * 28)

        @block.gpsimd
        def _(pool):
            pool.memset(ones[:, :], 1.0).then_inc(cst, 1)
            pool.memset(ident[:, :], 0.0).then_inc(cst, 1)
            pool.memset(negm[:, :], 0.0).then_inc(cst, 1)
            pool.memset(tri[:, :], 1.0).then_inc(cst, 1)
            pool.memset(lvl[:, :, :], 1.0).then_inc(cst, 1)
            pool.memset(maskb[:, :], NEG).then_inc(cst, 1)
            pool.memset(identb[:, :], 0.0).then_inc(cst, 1)
            pool.memset(epsc[:, 0:1], EPS).then_inc(cst, 1)
            pool.memset(epsc[:, 1:2], 1.0).then_inc(cst, 1)
            pool.wait_ge(cst, 9)
            pool.affine_select(out=ident[:, :], in_=ident[:, :], compare_op=ALU.not_equal, fill=1.0, base=0,
                               pattern=[[-1, 128]], channel_multiplier=1).then_inc(cst2, 1)
            pool.affine_select(out=identb[:, :], in_=identb[:, :], compare_op=ALU.not_equal, fill=1.0, base=0,
                               pattern=[[-1, 128]], channel_multiplier=1).then_inc(cst2, 1)
            pool.affine_select(out=tri[:, :], in_=tri[:, :], compare_op=ALU.is_ge, fill=0.0, base=0,
                               pattern=[[1, C]], channel_multiplier=-1).then_inc(cst2, 1)
            pool.affine_select(out=negm[:, :], in_=negm[:, :], compare_op=ALU.is_ge, fill=NEG, base=0,
                               pattern=[[1, C]], channel_multiplier=-1).then_inc(cst2, 1)
            pool.affine_select(out=maskb[:, :], in_=maskb[:, :], compare_op=ALU.is_ge, fill=0.0, base=0,
                               pattern=[[1, 128]], channel_multiplier=-1).then_inc(cst2, 1)
            n = 5
            for v in range(LEVELS):
                b = 1 << v
                for col0, cnt, w in level_blocks(b):
                    if w <= b:
                        pool.memset(lvl[:, v, col0:C], 0.0).then_inc(cst2, 1)
                        n += 1
                        continue
                    view = lvl[:, v, col0:col0 + cnt * w].rearrange("p (m w) -> p m w", w=w)
                    pool.affine_select(out=view, in_=view, compare_op=ALU.is_ge, fill=0.0, base=-col0,
                                       pattern=[[-2 * b, cnt], [0, w]], channel_multiplier=1).then_inc(cst2, 1)
                    pool.wait_ge(cst2, n + 1)
                    pool.affine_select(out=view, in_=view, compare_op=ALU.is_ge, fill=0.0, base=col0 + b - 1,
                                       pattern=[[2 * b, cnt], [0, w]], channel_multiplier=-1).then_inc(cst2, 1)
                    pool.wait_ge(cst2, n + 2)
                    pool.memset(view[:, :, 0:b], 0.0).then_inc(cst2, 1)
                    n += 3
            assert n == CONSTS, n
            pool.wait_ge(cst2, n)

            with pool.Fori(0, GH) as h:
                for s in range(4):
                    pool.wait_ge(ob, h * 3 + s + 1) if s < 3 else pool.wait_ge(taken, h * 12 + 12)
                    pool.dma_start(s_in_w[ds(h + s * 8, 1)].rearrange("t p c j -> p (t c) j"),
                                   obuf[:, s % 2, :].rearrange("p (c j) -> p c j", j=C)).then_inc(stored[s % 2], 16)

            pool.wait_ge(mm_chunk, P_GO.mm0)
            for b in range(2):
                pool.wait_ge(stored[b], 16 * 16)
            for g in range(2):
                pool.memset(B[g]["S"][:, :], 0.0).then_inc(c_s0, 1)
            pool.wait_ge(sml, SMALL)
            with pool.Fori(0, NC) as c:
                for g in range(2):
                    pool.wait_ge(cs["us"][g], c)
                    pool.wait_ge(cs["nt0"][g], c)
                    pool.wait_ge(cs["tg"][g], c)
                    pool.wait_ge(cs["nt"][g], c)
                    pool.wait_ge(cs["kde"][g], c * 2)
                pool.tensor_copy(cur[:, :], sm[:, ds(c, 1), :].rearrange("p a n -> p (a n)")).then_inc(c_cur, 1)
                pool.wait_ge(c_load, c * 16 + 16)
                pool.wait_ge(c_cur, c + 1)
                for g in range(2):
                    b, hs = B[g], slice(HG * g, HG * g + HG)
                    pool.wait_ge(cs["ss"][g], c)
                    pool.wait_ge(cs["oss"][g], c)
                    src = Xc[:, 0:16, :].rearrange("p (w h) j -> p w h j", w=2)[:, :, hs, :]
                    pool.tensor_tensor(b["sq"][:, :, :].rearrange("p w (h j) -> p w h j", h=HG), src, src,
                                       ALU.mult).then_inc(cs["sq"][g], 1)
                    pool.wait_ge(cs["gb"][g], c)
                    pool.tensor_tensor(b["tg"][:, :].rearrange("p (h j) -> p h j", h=HG),
                                       tri[:, :].unsqueeze(1).broadcast_to([C, HG, C]),
                                       cur[:, 32 + HG * g:32 + HG * g + HG].unsqueeze(2).broadcast_to([C, HG, C]),
                                       ALU.mult).then_inc(cs["tg"][g], 1)
                for g in range(2):
                    b = B[g]
                    d3 = b["dec"][0:C, :].rearrange("p (h j) -> p h j", h=HG)
                    pool.wait_ge(cs["dm"][g], c + 1)
                    pool.tensor_tensor(d3, d3, negm[:, :].unsqueeze(1).broadcast_to([C, HG, C]),
                                       ALU.add).then_inc(cs["dmm"][g], 1)
                for g in range(2):
                    b = B[g]
                    nt3 = b["NT"][:, :].rearrange("p (h j) -> p h j", h=HG)
                    pool.wait_ge(cs["nt0"][g], c + 1)
                    pool.tensor_tensor(nt3, nt3, cur[:, 8 + HG * g:8 + HG * g + HG].unsqueeze(2).broadcast_to([C, HG, C]),
                                       ALU.mult).then_inc(cs["nt"][g], 1)
                for v in range(LEVELS):
                    for g in range(2):
                        b = B[g]
                        if v == 0:
                            pool.wait_ge(cs["nt"][g], c + 1)
                        if v >= LTB:
                            if v == LTB:
                                pool.wait_ge(cs["t1p"][g], c + 1)
                                pool.wait_ge(cs["u1"][g], c + 1)
                            else:
                                pool.wait_ge(cs["x"][g], c * (LEVELS - 1) + (v - LTB))
                        pool.tensor_tensor(b["LT"][:, v % LTB, :].rearrange("p (h j) -> p h j", h=HG),
                                           b["NT"][:, :].rearrange("p (h j) -> p h j", h=HG),
                                           lvl[:, v, :].unsqueeze(1).broadcast_to([C, HG, C]),
                                           ALU.mult).then_inc(cs["lt"][g], 1)
                        if v == 2:
                            k3 = b["K"][:, :].rearrange("p (h d) -> p h d", h=HG)
                            pool.wait_ge(cs["kt"][g], c + 1)
                            pool.wait_ge(cs["dec"][g], c * 2 + 1)
                            pool.tensor_tensor(b["Kd"][:, :].rearrange("p (h d) -> p h d", h=HG), k3,
                                               b["kdx"][:, :].unsqueeze(2).broadcast_to([C, HG, 128]),
                                               ALU.mult).then_inc(cs["kde"][g], 1)
                            pool.tensor_tensor(b["Ke"][:, :].rearrange("p (h d) -> p h d", h=HG), k3,
                                               cur[:, 24 + HG * g:24 + HG * g + HG].unsqueeze(2).broadcast_to([C, HG, 128]),
                                               ALU.mult).then_inc(cs["kde"][g], 1)
                for g in range(2):
                    b = B[g]
                    pool.wait_ge(cs["op"][g], c + 1)
                    s3 = b["S"][:, :].rearrange("p (h d) -> p h d", h=HG)
                    egl = b["EG"][:, :].rearrange("p (h j) -> p h j", h=HG)[:, :, C - 1:C]
                    pool.tensor_tensor(s3, s3, egl.broadcast_to([128, HG, 128]), ALU.mult).then_inc(cs["sm2"][g], 1)
                for g in range(2):
                    b = B[g]
                    pool.wait_ge(cs["oc"][g], c + 1)
                    pool.tensor_tensor(b["sq"][:, 0, :], b["o"][:, :], b["o"][:, :], ALU.mult).then_inc(cs["osq"][g], 1)
            for g in range(2):
                pool.wait_ge(cs["ol"][g], NC)

            with pool.Fori(0, 4) as i:
                for s in range(4):
                    pool.wait_ge(taken, i * 12 + (TAKEN0[P_KV] + 3 * (s + 1)))
                    pool.dma_start(s_kv[ds(i * 4 + s, 1)].rearrange("a p n -> p (a n)"), obuf[:, s % 2, :]).then_inc(stored[s % 2], 16)
            with pool.Fori(0, 2) as i:
                for s in range(4):
                    pool.wait_ge(taken, i * 8 + (TAKEN0[P_Q] + 2 * (s + 1)))
                    pool.dma_start(s_q[ds(i * 4 + s, 1)].rearrange("a p n -> p (a n)"), obuf[:, s % 2, 0:SEQ]).then_inc(stored[s % 2], 16)
            for b in range(2):
                pool.wait_ge(stored[b], 16 * 28)
            pool.wait_ge(mm_chunk, P_O.mm0)
            for b in range(2):
                pool.memset(Pr[b][:, L:L + 1], 1.0).then_inc(t_one, 1)

        @block.scalar
        def _(act):
            def hi(s, count):
                act.wait_ge(raw_in[s], count)
                act.activation(WH[s][:, :], raw[s][:, :], ACT.Copy).then_inc(w_hi, 1)

            def norm(name, h_ready):
                chs, n0, _ = NORMS[name]
                for j, (t0, n) in enumerate(chs):
                    h_ready(act, j)
                    act.wait_ge(ss_r, n0 + j)
                    act.activation(sqb[:, :, 0:n], hT[:, :, t0:t0 + n], ACT.Square).then_inc(sq_r, 1)
                    act.wait_ge(ss_r, n0 + j + 1)
                    if n0 + j >= 2:
                        act.wait_ge(xn_r, n0 + j - 1)
                    r = rs[:, (n0 + j) % 2, 0:n]
                    act.activation(r, PS[:, j, 0:n], ACT.Ln, bias=epsc[:, 0:1], scale=1.0 / D).then_inc(ssln, 1)
                    act.wait_ge(ssln, n0 + j + 1)
                    act.activation(r, r, ACT.Exp, scale=-0.5).then_inc(r_r, 1)
                    act.wait_ge(xn_r, n0 + j + 1)
                    if name != "fin":
                        act.activation(XH[:, :, t0:t0 + n], xnb[:, :, 0:n], ACT.Copy).then_inc(xh_r, 1)

            for t in range(9):
                n = META if t == 8 else 128
                t0 = 0 if t == 8 else META + 128 * t
                act.wait_ge(x_tr, 2 * t + 1)
                act.activation(hT[:, 0:4, t0:t0 + n],
                               PS[:, 2 * (t % 3), :].rearrange("p (k n) -> p k n", k=4)[:, :, 0:n], ACT.Copy).then_inc(x_cpa, 1)
            act.wait_ge(x_cpa, 9)
            norm("gdn", lambda e, j: e.wait_ge(x_cpv, 9))
            act.wait_ge(ab_in, 16)
            act.activation(wabH[:, :, :], wab[:, :, :], ACT.Copy).then_inc(ab_h, 1)
            for s in range(4):
                hi(s, 16)
            act.wait_ge(xl_r, 3)

            def in_job(h, s, last):
                b = s % 2
                for ch, (t0, n) in enumerate(ALL_CH):
                    act.wait_ge(mm_chunk, h * 12 + (3 * s + ch + 1))
                    src = PS[:, 3 * b + ch, 0:n]
                    if s < 3:
                        act.activation(cin[:, 3 + t0:3 + t0 + n], src, ACT.Copy).then_inc(taken, 1)
                    else:
                        if ch == 0:
                            act.wait_ge(stored[1], h * 32 + 16)
                        act.activation(obuf[:, 1, t0:t0 + n], src, ACT.Silu).then_inc(taken, 1)
                if not last:
                    hi(s, h * 16 + 32)
                if s < 3:
                    act.wait_ge(conv, h * 12 + 4 * (s + 1))
                    act.wait_ge(stored[b], h * 32 + 16 * (s // 2))
                    act.activation(obuf[:, b, :], cac[:, :], ACT.Silu).then_inc(ob, 1)

            with act.Fori(0, GH - 1) as h:
                for s in range(4):
                    in_job(h, s, False)
            for s in range(4):
                in_job(GH - 1, s, True)

            act.wait_ge(c_dt, 32)
            act.wait_ge(sml, 2)
            act.activation(t80[1][:, :, :], t80[1][:, :, :], ACT.Exp, scale=-1.0).then_inc(sml, 1)
            act.activation(t80[2][:, :, :], ab[:, :, 8:16], ACT.Exp, scale=-1.0).then_inc(sml, 1)
            act.activation(alog[:, :], alog[:, :], ACT.Exp).then_inc(sml, 1)
            act.wait_ge(sml, 5)
            act.activation(t80[1][:, :, :], t80[1][:, :, :], ACT.Ln, bias=epsc[0:C, 1:2]).then_inc(sml, 1)
            act.wait_ge(sml, 13)
            act.activation(sm[:, :, 0:8], PS[0:C, 7, 0:8 * NC].rearrange("p (c h) -> p c h", h=8), ACT.Copy).then_inc(sml, 1)
            act.wait_ge(sml, 14)
            act.activation(t80[3][:, :, :], sm[:, :, 0:8], ACT.Exp).then_inc(sml, 1)
            with act.Fori(0, NC) as c:
                for g in range(2):
                    b = B[g]
                    act.wait_ge(cs["ss"][g], c + 1)
                    act.wait_ge(cs["on1"][g], c)
                    act.activation(b["rr"][:, :, :], PS[:, 4 * g:4 * g + 2, 0:GW], ACT.Ln, bias=epsc[:, 0:1]).then_inc(cs["rn"][g], 1)
                    act.wait_ge(cs["rn"][g], c * 2 + 1)
                    act.activation(b["rr"][:, :, :], b["rr"][:, :, :], ACT.Exp, scale=-0.5).then_inc(cs["rn"][g], 1)
                    act.wait_ge(cs["gb"][g], c + 1)
                    act.wait_ge(cs["sm2"][g], c)
                    act.activation(b["EG"][:, :], PS[:, 4 * g + 2, 0:GW], ACT.Exp).then_inc(cs["eg"][g], 1)
                for g in range(2):
                    b = B[g]
                    act.wait_ge(cs["dmm"][g], c + 1)
                    act.activation(b["kdx"][:, :], b["kdx"][:, :], ACT.Exp).then_inc(cs["dec"][g], 1)
                    act.activation(b["dec"][0:C, :], b["dec"][0:C, :], ACT.Exp).then_inc(cs["dec"][g], 1)
                for g in range(2):
                    b = B[g]
                    act.wait_ge(cs["tr"][g], c + 1)
                    act.activation(b["K"][:, :], PS[0:C, 4 * g + 2, :], ACT.Copy).then_inc(cs["kt"][g], 1)
                    act.activation(b["V"][:, :], PS[0:C, 4 * g + 3, :], ACT.Copy).then_inc(cs["vt"][g], 1)
                for v in range(LEVELS - 1):
                    for g in range(2):
                        b = B[g]
                        act.wait_ge(cs["x"][g], c * (LEVELS - 1) + v + 1)
                        act.activation(b["X"][:, :], PS[0:C, 4 * g + 1, 0:GW], ACT.Copy).then_inc(cs["xc"][g], 1)
                for g in range(2):
                    b = B[g]
                    act.wait_ge(cs["wt"][g], c + 1)
                    act.activation(b["WT"][:, :], PS[:, 4 * g, 0:GW], ACT.Copy).then_inc(cs["wtc"][g], 1)
                for g in range(2):
                    b = B[g]
                    act.wait_ge(cs["op"][g], c + 1)
                    act.activation(b["o"][:, :], PS[:, 4 * g + 2, 0:GW], ACT.Copy).then_inc(cs["oc"][g], 1)
                for g in range(2):
                    b = B[g]
                    act.wait_ge(cs["oss"][g], c + 1)
                    act.activation(b["rr"][:, 0, :], PS[:, 4 * g, 0:GW], ACT.Ln, bias=epsc[:, 0:1], scale=1.0 / GD).then_inc(cs["orn"][g], 1)
                    act.wait_ge(cs["orn"][g], c * 2 + 1)
                    act.activation(b["rr"][:, 0, :], b["rr"][:, 0, :], ACT.Exp, scale=-0.5).then_inc(cs["orn"][g], 1)
                for g in range(2):
                    b = B[g]
                    act.wait_ge(cs["on2"][g], c + 1)
                    act.activation(XH[:, HG * g:HG * g + HG, ds(c * C, C)],
                                   b["on"][:, :].rearrange("p (h j) -> p h j", h=HG), ACT.Copy).then_inc(cs["oh"][g], 1)
            for g in range(2):
                act.wait_ge(cs["ol"][g], NC)

            def first_splits(ph):
                act.wait_ge(mm_chunk, ph.mm0)
                for s in range(4):
                    hi(s, 16 * (ph.slot0[s] + 1))

            def next_split(ph, l):
                if l + 4 < ph.jobs:
                    act.wait_ge(mm_chunk, ph.mm0 + ph.nch * (l + 1))
                    hi(l % 4, 16 * (ph.slot0[l % 4] + l // 4 + 2))

            def ffn(ph, layer, name, h_ready):
                nch, chs = ph.nch, ph.chunks
                t00 = chs[0][0]
                W = chs[-1][0] + chs[-1][1] - t00
                DU = 8 * nch
                d0 = 24 * FG * layer
                a0 = 6 * FG * layer

                def activate(g, t):
                    for ch, (t0, n) in enumerate(chs):
                        act.wait_ge(mm_chunk, g * (4 * nch) + (ph.mm0 + 2 * nch * t + ch + 1))
                        if ch == 0:
                            act.wait_ge(act_a, g * (2 * nch) + (a0 + nch * t))
                        act.activation(gact[:, t0 - t00:t0 - t00 + n], PS[:, ch, 0:n], ACT.Silu).then_inc(silu_g, 1)
                    act.wait_ge(act_a, g * (2 * nch) + (a0 + nch * (t + 1)))
                    act.wait_ge(d_mm, g * DU + d0)
                    act.activation(AH[:, t, 0:W], aact[:, 0:W], ACT.Copy).then_inc(act_h, 1)

                def body(g, nxt):
                    activate(g, 0)
                    activate(g, 1)
                    if nxt:
                        for s in (1, 2, 3, 4):
                            act.wait_ge(mm_chunk, g * (4 * nch) + (ph.mm0 + nch * (s + 1)))
                            hi(s, g * 16 + 16 * (ph.slot0[s] + 2))
                        act.wait_ge(d_mm, g * DU + (d0 + DU))
                        hi(5, g * 16 + 16 * (ph.slot0[5] + 2))
                    if nxt == 1:
                        hi(0, g * 16 + 16 * (ph.slot0[0] + 3))

                act.wait_ge(mm_chunk, ph.mm0)
                hi(0, 16 * (ph.slot0[0] + 1))
                norm(name, h_ready)
                for s in range(1, 6):
                    hi(s, 16 * (ph.slot0[s] + 1))
                act.wait_ge(mm_chunk, ph.mm0 + nch)
                hi(0, 16 * (ph.slot0[0] + 2))
                act.wait_ge(xl_r, XL0[name] + len(NORMS[name][0]))
                with act.Fori(0, FG - 2) as g:
                    body(g, 1)
                body(FG - 2, 2)
                body(FG - 1, 0)

            first_splits(P_GO)
            for l in range(P_GO.jobs):
                next_split(P_GO, l)
            ffn(P_F0, 0, "f0", lambda e, j: e.wait_ge(taken, TAKEN0[P_GO] + P_GO.mm - 2 + j))

            def project(ph, name, tiles0):
                act.wait_ge(xl_r, XL0[name] + len(NORMS[name][0]))
                for l in range(ph.jobs):
                    b = l % 2
                    act.wait_ge(stored[b], 16 * ((tiles0 + l) // 2))
                    for ch, (t0, n) in enumerate(ph.chunks):
                        o0 = t0 - ph.chunks[0][0]
                        act.wait_ge(mm_chunk, ph.mm0 + ph.nch * l + ch + 1)
                        act.activation(obuf[:, b, o0:o0 + n], PS[:, ph.nch * b + ch, 0:n], ACT.Copy).then_inc(taken, 1)
                    next_split(ph, l)

            first_splits(P_KV)
            act.wait_ge(d_mm, 24 * FG)
            norm("kv", lambda e, j: e.wait_ge(d_add, 24 * (FG - 1) + 8 * (j + 1)))
            project(P_KV, "kv", 32)
            first_splits(P_Q)
            for b in range(2):
                act.wait_ge(stored[b], 16 * 24)
            norm("sb", lambda e, j: None)
            project(P_Q, "sb", 48)

            def attention_pair(i2, b):
                for j, (n0, nb) in enumerate(((0, 4), (4, 4), (8, 1))):
                    act.wait_ge(t_vt, i2 * 6 + (3 * b + j + 1))
                    rows = META if j == 2 else 128
                    act.activation(Vt[0:rows, n0:n0 + nb, :], PS[0:rows, 6, 0:128 * nb].rearrange("p (k n) -> p k n", n=128),
                                   ACT.Copy).then_inc(t_vc, 1)

                def sigmoids(u):
                    i, par = u // 2, u % 2
                    n = META + 128 * (i + 1)
                    z = PSf[:, 1536 * par + 496:1536 * par + 496 + n]
                    act.wait_ge(t_z, i2 * 32 + (16 * b + u + 1))
                    if u >= 2:
                        act.wait_ge(t_p, i2 * 32 + (16 * b + u - 1))
                    else:
                        act.wait_ge(t_p, i2 * 32 + 16 * b)
                    act.activation(kp[par][:, 0:n], z, ACT.Sigmoid, scale=-0.125).then_inc(t_kp, 1)
                    act.wait_ge(t_w, i2 * 32 + (16 * b + max(u - 1, 0)))
                    act.activation(sg[par][:, 0:n], z, ACT.Sigmoid, scale=0.125).then_inc(t_sg, 1)

                sigmoids(0)
                for u in range(2 * QB):
                    i, par = u // 2, u % 2
                    if u + 1 < 2 * QB:
                        sigmoids(u + 1)
                    for j, (k0, nb) in enumerate(tr_groups(i)):
                        act.wait_ge(t_tr, i2 * (2 * TRG) + (TRG * b + tr_before(u) + j + 1))
                        rows = META if k0 == 8 else 128
                        if j == 0 and u >= 2:
                            act.wait_ge(t_o, i2 * 32 + (16 * b + u - 1))
                        act.activation(wT[par][0:rows, k0:k0 + nb, :],
                                       PS[0:rows, 6, 0:128 * nb].rearrange("p (k n) -> p k n", n=128),
                                       ACT.Copy).then_inc(t_tc, 1)
                    if par:
                        act.wait_ge(t_o, i2 * 32 + (16 * b + u + 1))
                        act.activation(XH[:, ds(i2 * 2 + b, 1), META + 128 * i:META + 128 * (i + 1)].rearrange("p a n -> p (a n)"),
                                       PS[:, 7, 0:128], ACT.Copy).then_inc(t_oh, 1)
            PSf = PS[:, :, :].rearrange("p b n -> p (b n)")
            with act.Fori(0, PAIRS // 2) as i2:
                for b in range(2):
                    attention_pair(i2, b)
            act.wait_ge(t_ol, QB * PAIRS)

            first_splits(P_O)
            for l in range(P_O.jobs):
                next_split(P_O, l)
            ffn(P_F1, 1, "f1", lambda e, j: e.wait_ge(taken, TAKEN0[P_O] + P_O.mm))
            act.wait_ge(d_mm, 24 * FG + 16 * FG)
            norm("fin", lambda e, j: e.wait_ge(d_add, 24 * FG + 16 * (FG - 1) + 8 * (j // 2 + 1)))
            for t in range(QB):
                act.wait_ge(o_tr, 2 * t + 1)
                if t >= 2:
                    act.wait_ge(o_out[t % 2], 16 * (t // 2))
                act.activation(fo[:, t % 2, 0:512], PS[:, 4 + 2 * (t % 2), :], ACT.Copy).then_inc(o_cpa, 1)

        @block.vector
        def _(dve):
            own = {"n": 0}

            def norm(name):
                chs, n0, col = NORMS[name]
                for j, (t0, n) in enumerate(chs):
                    dve.wait_ge(r_r, n0 + j + 1)
                    if name != "fin" and n0 + j:
                        dve.wait_ge(xl_r, n0 + j)
                        dve.wait_ge(xh_r, n0 + j)
                    if name == "fin":
                        for m in range(KT):
                            dst = hT[:, m, t0:t0 + n]
                            x_ = dve.scalar_tensor_tensor(dst, hT[:, m, t0:t0 + n], pvec[:, col + m:col + m + 1],
                                                          rs[:, (n0 + j) % 2, 0:n], ALU.mult, ALU.mult)
                        x_.then_inc(xn_r, 1)
                        continue
                    for m in range(KT):
                        x_ = dve.scalar_tensor_tensor(xnb[:, m, 0:n], hT[:, m, t0:t0 + n], pvec[:, col + m:col + m + 1],
                                                      rs[:, (n0 + j) % 2, 0:n], ALU.mult, ALU.mult)
                    x_.then_inc(xn_r, 1)
                    dve.wait_ge(xh_r, n0 + j + 1)
                    dve.wait_ge(xn_r, n0 + j + 1)
                    dve.tensor_tensor(XL[:, :, t0:t0 + n], xnb[:, :, 0:n], XH[:, :, t0:t0 + n].bitcast(F32),
                                      ALU.subtract).then_inc(xl_r, 1)

            def lo(s, count):
                dve.wait_ge(w_hi, count)
                dve.tensor_tensor(WL[s][:, :], raw[s][:, :], WH[s][:, :].bitcast(F32), ALU.subtract).then_inc(w_lo, 1)

            for t in range(9):
                n = META if t == 8 else 128
                t0 = 0 if t == 8 else META + 128 * t
                dve.wait_ge(x_tr, 2 * t + 2)
                dve.tensor_copy(hT[:, 4:8, t0:t0 + n],
                                PS[:, 2 * (t % 3) + 1, :].rearrange("p (k n) -> p k n", k=4)[:, :, 0:n]).then_inc(x_cpv, 1)
            dve.wait_ge(p_tr, 2)
            dve.tensor_copy(pvec[:, 0:121], PS[:, 6, 0:121]).then_inc(p_cp, 1)
            dve.tensor_copy(pvec[:, 121:145], PS[:, 7, 0:24]).then_inc(p_cp, 1)
            dve.wait_ge(p_cp, 2)
            norm("gdn")
            dve.wait_ge(ab_h, 1)
            dve.tensor_tensor(wabL[:, :, :], wab[:, :, :], wabH[:, :, :].bitcast(F32), ALU.subtract).then_inc(ab_l, 1)
            for s in range(4):
                lo(s, s + 1)
            dve.wait_ge(xh_r, 3)
            dve.wait_ge(xl_r, 3)
            dve.memset(cin[:, 0:3], 0.0).then_inc(cin0, 1)
            dve.wait_ge(ab_mm, 1)
            dve.tensor_copy(ab[:, :, :], PS[0:C, 6, 0:16 * NC].rearrange("p (c n) -> p c n", n=16)).then_inc(ab_cp, 1)

            def in_job(h, s, last):
                if s < 3:
                    dve.wait_ge(taken, h * 12 + (3 * s + 3))
                    dve.wait_ge(ob, h * 3 + s)
                    dve.wait_ge(cin0, 1)
                    for i in range(4):
                        w = pvec[:, ds(h + (CONV + 24 * i + 8 * s), 1)]
                        dve.wait_ge(conv, h * 12 + (4 * s + i))
                        if i == 0:
                            y = dve.tensor_scalar(cac[:, :], cin[:, 0:L], w, None, ALU.mult)
                        else:
                            y = dve.scalar_tensor_tensor(cac[:, :], cin[:, i:i + L], w, cac[:, :], ALU.mult, ALU.add)
                        y.then_inc(conv, 1)
                if not last:
                    lo(s, h * 4 + (s + 5))
            with dve.Fori(0, GH - 1) as h:
                for s in range(4):
                    in_job(h, s, False)
            for s in range(4):
                in_job(GH - 1, s, True)

            a3, b3 = ab[:, :, 0:8], ab[:, :, 8:16]
            dve.wait_ge(c_dt, 32)
            dve.wait_ge(ab_cp, 1)
            dve.tensor_tensor(t80[0][:, :, :], a3, dtb[:, :].unsqueeze(1).broadcast_to([C, NC, 8]), ALU.add).then_inc(sml, 1)
            dve.wait_ge(sml, 1)
            dve.scalar_tensor_tensor(t80[1][:, :, :], t80[0][:, :, :], -1.0, t80[0][:, :, :], ALU.mult, ALU.max).then_inc(sml, 1)
            dve.wait_ge(sml, 6)
            dve.tensor_scalar(t80[0][:, :, :], t80[0][:, :, :], 0.0, None, ALU.max).then_inc(sml, 1)
            dve.wait_ge(sml, 7)
            dve.tensor_tensor(t80[0][:, :, :], t80[0][:, :, :], t80[1][:, :, :], ALU.add).then_inc(sml, 1)
            dve.tensor_scalar(t80[2][:, :, :], t80[2][:, :, :], 1.0, None, ALU.add).then_inc(sml, 1)
            dve.wait_ge(sml, 9)
            dve.scalar_tensor_tensor(sm[:, :, 32:40], t80[0][:, :, :], -1.0, alog[:, :].unsqueeze(1).broadcast_to([C, NC, 8]),
                                     ALU.mult, ALU.mult).then_inc(sml, 1)
            dve.reciprocal(sm[:, :, 16:24], t80[2][:, :, :]).then_inc(sml, 1)
            dve.wait_ge(sml, 11)
            dve.tensor_scalar(sm[:, :, 8:16], sm[:, :, 16:24], -1.0, None, ALU.mult).then_inc(sml, 1)
            dve.wait_ge(sml, 15)
            dve.tensor_scalar(sm[:, :, 24:32], t80[3][:, :, :], -1.0, None, ALU.mult).then_inc(sml, 1)
            with dve.Fori(0, NC) as c:
                dve.wait_ge(c_cur, c + 1)
                dve.wait_ge(c_load, c * 16 + 16)
                for g in range(2):
                    b = B[g]
                    h4 = dict(h=HG)
                    v3 = lambda t: t.rearrange("p (h j) -> p h j", h=HG)
                    q3 = Xc[:, HG * g:HG * g + HG, :].rearrange("p h j -> p (h j)")
                    k3 = Xc[:, 8 + HG * g:8 + HG * g + HG, :].rearrange("p h j -> p (h j)")
                    dve.wait_ge(cs["eg"][g], c + 1)
                    gj = cur[:, HG * g:HG * g + HG].unsqueeze(2)
                    gb = v3(PS[0:C, 4 * g + 2, 0:GW])
                    dve.tensor_tensor(v3(b["dec"][0:C, :]), gb, gj.broadcast_to([C, HG, C]), ALU.subtract)
                    dve.tensor_tensor(b["kdx"][:, :].unsqueeze(2), gb[:, :, C - 1:C], gj, ALU.subtract).then_inc(cs["dm"][g], 1)
                    dve.wait_ge(cs["rn"][g], c * 2 + 2)
                    dve.tensor_tensor(b["KQ"][:, 0, :], k3, b["rr"][:, 1, :], ALU.mult)
                    dve.scalar_tensor_tensor(b["KQ"][:, 1, :], q3, GD ** -0.5, b["rr"][:, 0, :], ALU.mult, ALU.mult).then_inc(cs["kn"][g], 1)
                    dve.wait_ge(cs["kn"][g], c + 1)
                    dve.wait_ge(cs["eg"][g], c + 1)
                    dve.tensor_tensor(b["Qd"][:, :], b["KQ"][:, 1, :], b["EG"][:, :], ALU.mult).then_inc(cs["qd"][g], 1)
                for g in range(2):
                    b = B[g]
                    dve.wait_ge(cs["dec"][g], c * 2 + 2)
                    dve.wait_ge(cs["kk"][g], c + 1)
                    dve.wait_ge(cs["lt"][g], c * LEVELS)
                    dve.tensor_tensor(b["NT"][:, :], PS[0:C, 4 * g, 0:GW], b["dec"][0:C, :], ALU.mult).then_inc(cs["nt0"][g], 1)
                    dve.tensor_tensor(b["attn"][:, :], PS[0:C, 4 * g + 1, 0:GW], b["dec"][0:C, :], ALU.mult).then_inc(cs["att"][g], 1)
                idb = ident[0:C, 0:C].unsqueeze(1).broadcast_to([C, HG, C])
                for g in range(2):
                    b = B[g]
                    dve.wait_ge(cs["lt"][g], c * LEVELS + 1)
                    dve.tensor_tensor(v3(b["U"][:, :]), v3(b["LT"][:, 0, :]), idb, ALU.add).then_inc(cs["u1"][g], 1)
                for g in range(2):
                    b = B[g]
                    dve.wait_ge(cs["t1p"][g], c + 1)
                    dve.tensor_tensor(v3(b["T"][:, :]), v3(PS[0:C, 4 * g, 0:GW]), idb, ALU.add).then_inc(cs["t1"][g], 1)
                for v in range(LEVELS - 1):
                    for g in range(2):
                        b = B[g]
                        dve.wait_ge(cs["tu"][g], c * (LEVELS - 1) + v + 1)
                        dve.wait_ge(cs["t1"][g], c + 1)
                        if v < LEVELS - 2:
                            dve.tensor_tensor(b["T"][:, :], PS[0:C, 4 * g + 2, 0:GW], b["T"][:, :], ALU.add)
                        dve.tensor_tensor(b["U"][:, :], PS[0:C, 4 * g + 3, 0:GW], b["U"][:, :], ALU.add).then_inc(cs["u"][g], 1)
                        if v < LEVELS - 2:
                            dve.wait_ge(cs["u"][g], c * (LEVELS - 1) + v + 1)
                for g in range(2):
                    b = B[g]
                    dve.wait_ge(cs["up"][g], c + 1)
                    dve.tensor_tensor(b["u"][:, :].rearrange("p (h d) -> p h d", h=HG),
                                      PS[0:C, 4 * g + 1, :].rearrange("p (h d) -> p h d", h=HG),
                                      cur[:, 16 + HG * g:16 + HG * g + HG].unsqueeze(2).broadcast_to([C, HG, 128]),
                                      ALU.mult).then_inc(cs["us"][g], 1)
                for g in range(2):
                    b = B[g]
                    dve.wait_ge(cs["sm2"][g], c + 1)
                    dve.wait_ge(cs["sp"][g], c + 1)
                    dve.tensor_tensor(b["S"][:, :], PS[:, 4 * g + 3, :], b["S"][:, :], ALU.add).then_inc(cs["snew"][g], 1)
                dve.wait_ge(c_gate, c * 16 + 16)
                for g in range(2):
                    b = B[g]
                    dve.wait_ge(cs["orn"][g], c * 2 + 2)
                    dve.wait_ge(cs["oc"][g], c + 1)
                    dve.tensor_tensor(b["on"][:, :], b["o"][:, :], b["rr"][:, 0, :], ALU.mult).then_inc(cs["on1"][g], 1)
                    dve.wait_ge(cs["on1"][g], c + 1)
                    dve.scalar_tensor_tensor(b["on"][:, :], b["on"][:, :], pvec[:, ON:ON + 1],
                                             Gt[:, HG * g:HG * g + HG, :].rearrange("p h j -> p (h j)"),
                                             ALU.mult, ALU.mult).then_inc(cs["on2"][g], 1)
                for g in range(2):
                    b = B[g]
                    dve.wait_ge(cs["on2"][g], c + 1)
                    dve.wait_ge(cs["oh"][g], c + 1)
                    dst = slice(HG * g, HG * g + HG)
                    dve.tensor_tensor(XL[:, dst, ds(c * C, C)], v3(b["on"][:, :]),
                                      XH[:, dst, ds(c * C, C)].bitcast(F32), ALU.subtract).then_inc(cs["ol"][g], 1)

            def add_phase(ph):
                for s in range(4):
                    lo(s, ph.job0 + s + 1)
                for l in range(ph.jobs):
                    for ch, (t0, n) in enumerate(ph.chunks):
                        dve.wait_ge(mm_chunk, ph.mm0 + ph.nch * l + ch + 1)
                        dst = hT[:, l, t0:t0 + n]
                        dve.tensor_tensor(dst, PS[:, ph.nch * (l % 2) + ch, 0:n], dst, ALU.add).then_inc(taken, 1)
                    if l + 4 < ph.jobs:
                        lo(l % 4, ph.job0 + l + 5)

            def ffn(ph, layer):
                nch, chs = ph.nch, ph.chunks
                t00 = chs[0][0]
                W = chs[-1][0] + chs[-1][1] - t00
                DU = 8 * nch
                d0 = 0 if layer == 0 else 24 * FG
                a0 = 0 if layer == 0 else 6 * FG
                banks = down_banks(nch)
                lo(0, ph.job0 + 1)
                norm("f0" if layer == 0 else "f1")
                for s in range(1, 6):
                    lo(s, ph.job0 + s + 1)
                lo(0, ph.job0 + 7)

                def tile(g, t):
                    for ch, (t0, n) in enumerate(chs):
                        dve.wait_ge(silu_g, g * (2 * nch) + (a0 + nch * t + ch + 1))
                        dve.wait_ge(mm_chunk, g * (4 * nch) + (ph.mm0 + nch * (2 * t + 1) + ch + 1))
                        if ch == 0:
                            dve.wait_ge(act_h, g * 2 + (t + 2 * FG * layer))
                            dve.wait_ge(act_l, g * 2 + (t + 2 * FG * layer))
                        o = slice(t0 - t00, t0 - t00 + n)
                        dve.tensor_tensor(aact[:, o], PS[:, nch + ch, 0:n], gact[:, o], ALU.mult).then_inc(act_a, 1)
                    dve.wait_ge(act_h, g * 2 + (t + 1 + 2 * FG * layer))
                    dve.wait_ge(act_a, g * (2 * nch) + (a0 + nch * (t + 1)))
                    dve.tensor_tensor(AL[:, t, 0:W], aact[:, 0:W], AH[:, t, 0:W].bitcast(F32), ALU.subtract).then_inc(act_l, 1)

                def body(g, nxt):
                    j = ph.job0 + 7
                    tile(g, 0)
                    tile(g, 1)
                    if nxt:
                        for k, s in enumerate((1, 2, 3, 4)):
                            lo(s, g * 6 + (j + k + 1))
                    for u in range(DU):
                        ch, m = u // 8, u % 8
                        t0, n = chs[ch]
                        dve.wait_ge(d_mm, g * DU + (d0 + u + 1))
                        if u == 0:
                            dve.wait_ge(d_add, g * DU + d0)
                        dst = hT[:, m, t0:t0 + n]
                        dve.tensor_tensor(dst, PS[:, banks[u % len(banks)], 0:n], dst, ALU.add).then_inc(d_add, 1)
                    if nxt:
                        lo(5, g * 6 + (j + 5))
                    if nxt == 1:
                        lo(0, g * 6 + (j + 6))
                with dve.Fori(0, FG - 2) as g:
                    body(g, 1)
                body(FG - 2, 2)
                body(FG - 1, 0)

            for g in range(2):
                dve.wait_ge(cs["ol"][g], NC)
            add_phase(P_GO)
            ffn(P_F0, 0)
            for s in range(4):
                lo(s, P_KV.job0 + s + 1)
            norm("kv")
            for l in range(P_KV.jobs - 4):
                lo(l % 4, P_KV.job0 + l + 5)
            for s in range(4):
                lo(s, P_Q.job0 + s + 1)
            norm("sb")
            for l in range(P_Q.jobs - 4):
                lo(l % 4, P_Q.job0 + l + 5)

            dve.wait_ge(t_one, 2)
            def attention_pair(i2, b):
                for u in range(2 * QB):
                    i, par = u // 2, u % 2
                    n = META + 128 * (i + 1)
                    k = i2 * 32 + (16 * b + u)
                    dve.wait_ge(t_kp, k + 1)
                    Pv = Pr[par][:, L - n:L]
                    dve.wait_ge(t_w, k)
                    dve.tensor_tensor_scan(Pv[:, ::-1], kp[par][:, 0:n][:, ::-1], kp[par][:, 0:n][:, ::-1], 1.0,
                                           ALU.mult, ALU.bypass).then_inc(t_p, 1)
                    dve.wait_ge(t_p, k + 1)
                    dve.wait_ge(t_sg, k + 1)
                    if u >= 2:
                        dve.wait_ge(t_tr, i2 * (2 * TRG) + (TRG * b + tr_before(u - 1)))
                    else:
                        dve.wait_ge(t_tr, i2 * (2 * TRG) + TRG * b)
                    dve.tensor_tensor(wt[par][:, 0:n], Pr[par][:, L - n + 1:L + 1], sg[par][:, 0:n], ALU.mult).then_inc(t_w, 1)
                    if u >= 2 and par == 0:
                        finish(i2, b, i - 1)
                finish(i2, b, QB - 1)

            def finish(i2, b, i):
                dve.wait_ge(t_oh, i2 * 16 + (8 * b + i + 1))
                cols = slice(META + 128 * i, META + 128 * (i + 1))
                dve.tensor_tensor(XL[:, ds(i2 * 2 + b, 1), cols].rearrange("p a n -> p (a n)"), PS[:, 7, 0:128],
                                  XH[:, ds(i2 * 2 + b, 1), cols].rearrange("p a n -> p (a n)").bitcast(F32),
                                  ALU.subtract).then_inc(t_ol, 1)
            with dve.Fori(0, PAIRS // 2) as i2:
                for b in range(2):
                    attention_pair(i2, b)

            add_phase(P_O)
            ffn(P_F1, 1)
            norm("fin")
            for t in range(QB):
                dve.wait_ge(o_tr, 2 * t + 2)
                if t >= 2:
                    dve.wait_ge(o_out[t % 2], 16 * (t // 2))
                dve.tensor_copy(fo[:, t % 2, 512:1024], PS[:, 5 + 2 * (t % 2), :]).then_inc(o_cpv, 1)

        @block.tensor
        def _(pe):
            def norm(name):
                chs, n0, _ = NORMS[name]
                for j, (t0, n) in enumerate(chs):
                    pe.wait_ge(sq_r, n0 + j + 1)
                    for k in range(KT):
                        m = pe.matmul(PS[:, j, 0:n], ones[:, :], sqb[:, k, 0:n], start=(k == 0), stop=(k == KT - 1))
                    m.then_inc(ss_r, 1)

            def chunk(s, bank, t0, n):
                for k in range(KT):
                    wh, wl = WH[s][:, 128 * k:128 * k + 128], WL[s][:, 128 * k:128 * k + 128]
                    xh, xl = XH[:, k, t0:t0 + n], XL[:, k, t0:t0 + n]
                    pe.matmul(PS[:, bank, 0:n], wl, xh, start=(k == 0), stop=False)
                    pe.matmul(PS[:, bank, 0:n], wh, xl, start=False, stop=False)
                    m = pe.matmul(PS[:, bank, 0:n], wh, xh, start=False, stop=(k == KT - 1))
                m.then_inc(mm_chunk, 1)

            pe.wait_ge(cst2, CONSTS)
            pe.wait_ge(x_in, 32)
            for t in range(9):
                n = META if t == 8 else 128
                if t >= 3:
                    pe.wait_ge(x_cpa, t - 2)
                    pe.wait_ge(x_cpv, t - 2)
                for half in range(2):
                    for k in range(4):
                        f = 4 * half + k
                        m = pe.transpose(PS[:, 2 * (t % 3) + half, 128 * k:128 * k + n], xin[0:n, t, 128 * f:128 * f + 128],
                                         ident[0:n, 0:n])
                    m.then_inc(x_tr, 1)
            pe.wait_ge(p_in, 16 * 7)
            pe.transpose(PS[:, 6, 0:121], prow[0:121, :], ident[0:121, 0:121]).then_inc(p_tr, 1)
            pe.transpose(PS[:, 7, 0:24], prow2[:, :], ident[0:24, 0:24]).then_inc(p_tr, 1)
            pe.wait_ge(x_cpa, 9)
            pe.wait_ge(x_cpv, 9)
            norm("gdn")
            pe.wait_ge(ab_l, 1)
            pe.wait_ge(p_cp, 2)
            pe.wait_ge(xl_r, 3)
            for c in range(NC):
                for k in range(KT):
                    xh, xl = XH[:, k, c * C:(c + 1) * C], XL[:, k, c * C:(c + 1) * C]
                    o = PS[0:C, 6, 16 * c:16 * c + 16]
                    pe.matmul(o, xl, wabH[:, k, :], start=(k == 0), stop=False)
                    pe.matmul(o, xh, wabL[:, k, :], start=False, stop=False)
                    m = pe.matmul(o, xh, wabH[:, k, :], start=False, stop=(k == KT - 1))
            m.then_inc(ab_mm, 1)

            with pe.Fori(0, GH) as h:
                for s in range(4):
                    pe.wait_ge(w_lo, h * 4 + s + 1)
                    for ch, (t0, n) in enumerate(ALL_CH):
                        if s >= 2:
                            pe.wait_ge(taken, h * 12 + (3 * s + ch - 5))
                        else:
                            pe.wait_ge(taken, h * 12)
                        chunk(s, 3 * (s % 2) + ch, t0, n)

            pe.wait_ge(sml, 12)
            pe.matmul(PS[0:C, 7, 0:8 * NC], tri[:, :], sm[:, :, 32:40], start=True, stop=True).then_inc(sml, 1)
            pe.wait_ge(sml, SMALL)
            pe.wait_ge(c_s0, 2)

            def hd(t, h, w=C):
                return t[:, h * w:(h + 1) * w]

            with pe.Fori(0, NC) as c:
                for g in range(2):
                    b, p0 = B[g], 4 * g
                    pe.wait_ge(cs["sq"][g], c + 1)
                    pe.wait_ge(cs["orn"][g], c * 2)
                    pe.wait_ge(cs["us"][g], c)
                    pe.matmul(PS[:, p0, 0:GW], ones[:, :], b["sq"][:, 0, :], start=True, stop=True)
                    pe.matmul(PS[:, p0 + 1, 0:GW], ones[:, :], b["sq"][:, 1, :], start=True, stop=True).then_inc(cs["ss"][g], 1)
                    pe.wait_ge(cs["tg"][g], c + 1)
                    pe.wait_ge(cs["oc"][g], c)
                    pe.matmul(PS[:, p0 + 2, 0:GW], ones[0:C, :], b["tg"][:, :], start=True, stop=True).then_inc(cs["gb"][g], 1)
                for g in range(2):
                    b, p0 = B[g], 4 * g
                    pe.wait_ge(cs["kn"][g], c + 1)
                    for h in range(HG):
                        pe.matmul(PS[0:C, p0, h * C:(h + 1) * C], hd(b["KQ"][:, 0, :], h), hd(b["KQ"][:, 0, :], h), start=True, stop=True)
                    for h in range(HG):
                        m = pe.matmul(PS[0:C, p0 + 1, h * C:(h + 1) * C], hd(b["KQ"][:, 0, :], h), hd(b["KQ"][:, 1, :], h), start=True, stop=True)
                    m.then_inc(cs["kk"][g], 1)
                    pe.wait_ge(cs["dm"][g], c + 1)
                    pe.wait_ge(cs["eg"][g], c + 1)
                    pe.wait_ge(cs["snew"][g], c)
                    for h in range(HG):
                        pe.transpose(PS[0:C, p0 + 2, h * 128:(h + 1) * 128], hd(b["KQ"][:, 0, :], h), ident[:, :])
                    for h in range(HG):
                        m = pe.transpose(PS[0:C, p0 + 3, h * 128:(h + 1) * 128], Xc[:, 16 + HG * g + h, :], ident[:, :])
                    m.then_inc(cs["tr"][g], 1)
                for g in range(2):
                    b, p0 = B[g], 4 * g
                    pe.wait_ge(cs["lt"][g], c * LEVELS + 1)
                    pe.wait_ge(cs["nt0"][g], c + 1)
                    for h in range(HG):
                        m = pe.transpose(PS[0:C, p0, h * C:(h + 1) * C], hd(b["LT"][:, 0, :], h), ident[0:C, 0:C])
                    m.then_inc(cs["t1p"][g], 1)
                for v in range(LEVELS - 1):
                    for g in range(2):
                        b, p0 = B[g], 4 * g
                        if v == 0:
                            pe.wait_ge(cs["t1"][g], c + 1)
                            pe.wait_ge(cs["u1"][g], c + 1)
                            pe.wait_ge(cs["att"][g], c + 1)
                            pe.wait_ge(cs["kt"][g], c + 1)
                            pe.wait_ge(cs["vt"][g], c + 1)
                        else:
                            pe.wait_ge(cs["u"][g], c * (LEVELS - 1) + v)
                        pe.wait_ge(cs["lt"][g], c * LEVELS + (v + 2))
                        pe.wait_ge(cs["xc"][g], c * (LEVELS - 1) + v)
                        for h in range(HG):
                            m = pe.matmul(PS[0:C, p0 + 1, h * C:(h + 1) * C], hd(b["LT"][:, (v + 1) % LTB, :], h), hd(b["T"], h), start=True, stop=True)
                        m.then_inc(cs["x"][g], 1)
                    for g in range(2):
                        b, p0 = B[g], 4 * g
                        pe.wait_ge(cs["xc"][g], c * (LEVELS - 1) + (v + 1))
                        for h in range(HG):
                            if v < LEVELS - 2:
                                pe.matmul(PS[0:C, p0 + 2, h * C:(h + 1) * C], hd(b["U"], h), hd(b["X"], h), start=True, stop=True)
                        for h in range(HG):
                            m = pe.matmul(PS[0:C, p0 + 3, h * C:(h + 1) * C], hd(b["X"], h), hd(b["U"], h), start=True, stop=True)
                        m.then_inc(cs["tu"][g], 1)
                for g in range(2):
                    b, p0 = B[g], 4 * g
                    pe.wait_ge(cs["u"][g], c * (LEVELS - 1) + (LEVELS - 1))
                    pe.wait_ge(cs["kde"][g], c * 2 + 2)
                    for h in range(HG):
                        m = pe.matmul(PS[:, p0, h * C:(h + 1) * C], hd(b["Ke"], h, 128), hd(b["U"], h), start=True, stop=True)
                    m.then_inc(cs["wt"][g], 1)
                for g in range(2):
                    b, p0 = B[g], 4 * g
                    pe.wait_ge(cs["wtc"][g], c + 1)
                    pe.wait_ge(cs["snew"][g], c)
                    for h in range(HG):
                        o = PS[0:C, p0 + 1, h * 128:(h + 1) * 128]
                        pe.matmul(o, hd(b["U"], h), hd(b["V"], h, 128), start=True, stop=False)
                        m = pe.matmul(o, hd(b["WT"], h), hd(b["S"], h, 128), start=False, stop=True)
                    m.then_inc(cs["up"][g], 1)
                for g in range(2):
                    b, p0 = B[g], 4 * g
                    pe.wait_ge(cs["us"][g], c + 1)
                    pe.wait_ge(cs["qd"][g], c + 1)
                    for h in range(HG):
                        o = PS[:, p0 + 2, h * C:(h + 1) * C]
                        pe.matmul(o, hd(b["S"], h, 128), hd(b["Qd"], h), start=True, stop=False)
                        m = pe.matmul(o, hd(b["u"], h, 128), hd(b["attn"], h), start=False, stop=True)
                    m.then_inc(cs["op"][g], 1)
                    for h in range(HG):
                        m = pe.matmul(PS[:, p0 + 3, h * 128:(h + 1) * 128], hd(b["Kd"], h, 128), hd(b["u"], h, 128), start=True, stop=True)
                    m.then_inc(cs["sp"][g], 1)
                for g in range(2):
                    b, p0 = B[g], 4 * g
                    pe.wait_ge(cs["osq"][g], c + 1)
                    pe.matmul(PS[:, p0, 0:GW], ones[:, :], b["sq"][:, 0, :], start=True, stop=True).then_inc(cs["oss"][g], 1)
            for g in range(2):
                pe.wait_ge(cs["ol"][g], NC)

            def dense(ph, norm_name):
                t_base = TAKEN0[ph]
                for l in range(ph.jobs):
                    s = l % 4
                    pe.wait_ge(w_lo, ph.job0 + l + 1)
                    for ch, (t0, n) in enumerate(ph.chunks):
                        if l == 0 and norm_name:
                            pe.wait_ge(xl_r, xn_needed(norm_name, ph, ch))
                        if l >= 2:
                            pe.wait_ge(taken, t_base + ph.nch * (l - 2) + ch + 1)
                        chunk(s, ph.nch * (l % 2) + ch, t0, n)

            def ffn(ph, layer, name):
                nch, chs = ph.nch, ph.chunks
                DU = 8 * nch
                d0 = 0 if layer == 0 else 24 * FG
                s0 = 0 if layer == 0 else 6 * FG
                banks = down_banks(nch)
                t00 = chs[0][0]
                pe.wait_ge(w_lo, ph.job0 + 1)
                for ch, (t0, n) in enumerate(chs):
                    pe.wait_ge(xl_r, xn_needed(name, ph, ch))
                    chunk(0, ch, t0, n)

                def down(g, sa, sb):
                    pe.wait_ge(act_l, g * 2 + (2 + 2 * FG * layer))
                    for u in range(DU):
                        ch, m = u // 8, u % 8
                        t0, n = chs[ch]
                        bank = PS[:, banks[u % len(banks)], 0:n]
                        if u >= len(banks):
                            pe.wait_ge(d_add, g * DU + (d0 + u - len(banks) + 1))
                        for t, s in ((0, sa), (1, sb)):
                            wh, wl = WH[s][:, 128 * m:128 * m + 128], WL[s][:, 128 * m:128 * m + 128]
                            ah, al = AH[:, t, t0 - t00:t0 - t00 + n], AL[:, t, t0 - t00:t0 - t00 + n]
                            pe.matmul(bank, wl, ah, start=(t == 0), stop=False)
                            pe.matmul(bank, wh, al, start=False, stop=False)
                            y = pe.matmul(bank, wh, ah, start=False, stop=(t == 1))
                        y.then_inc(d_mm, 1)

                def body(g, last):
                    j = ph.job0 + 1
                    for k, (s, bank0) in enumerate(((1, nch), (2, 0), (3, nch), (4, 0))):
                        if k == 3 and last:
                            break
                        pe.wait_ge(w_lo, g * 6 + (j + k + 1))
                        if k == 0:
                            pe.wait_ge(d_add, g * DU + d0)
                        if k == 1:
                            pe.wait_ge(silu_g, g * (2 * nch) + (s0 + nch))
                        if k == 2:
                            pe.wait_ge(act_a, g * (2 * nch) + (s0 + nch))
                        if k == 3:
                            pe.wait_ge(silu_g, g * (2 * nch) + (s0 + 2 * nch))
                        for ch, (t0, n) in enumerate(chs):
                            chunk(s, bank0 + ch, t0, n)
                    if last:
                        pe.wait_ge(w_lo, g * 6 + (j + 5))
                        down(g, 4, 5)
                    else:
                        pe.wait_ge(w_lo, g * 6 + (j + 6))
                        down(g, 5, 0)
                with pe.Fori(0, FG - 1) as g:
                    body(g, False)
                body(FG - 1, True)

            dense(P_GO, None)
            norm("f0")
            ffn(P_F0, 0, "f0")
            norm("kv")
            dense(P_KV, "kv")
            norm("sb")
            dense(P_Q, "sb")

            PSf = PS[:, :, :].rearrange("p b n -> p (b n)")
            pe.wait_ge(taken, TAKEN0[P_O])

            def attention_pair(i2, b):
                K, Q = kq[b][:, 0:L], kq[b][:, L:L + SEQ]
                pe.wait_ge(t_load[b], i2 * 48 + 48)
                pe.wait_ge(t_ol, i2 * 16 + 8 * b)
                for j, blocks in enumerate((range(0, 4), range(4, 8), (8,))):
                    pe.wait_ge(t_vc, i2 * 6 + (3 * b + j))
                    if j == 0:
                        pe.wait_ge(t_tc, i2 * (2 * TRG) + TRG * b)
                    for k in blocks:
                        n, t0 = (META, 0) if k == 8 else (128, META + 128 * k)
                        m = pe.transpose(PS[0:n, 6, 128 * (k % 4):128 * (k % 4) + 128], vT[b][:, t0:t0 + n], ident[:, :])
                    m.then_inc(t_vt, 1)

                def scores(u):
                    i, par = u // 2, u % 2
                    rows = slice(64 * par, 64 * par + 64)
                    q = Q[rows, 128 * i:128 * i + 128]
                    z0 = 1536 * par + 496
                    pe.wait_ge(t_sg, i2 * 32 + (16 * b + max(u - 1, 0)))
                    pe.matmul(PSf[:, z0:z0 + META], q, K[rows, 0:META], start=True, stop=True)
                    for k0 in range(0, i + 1, 4):
                        nb = min(4, i + 1 - k0)
                        last = k0 + nb == i + 1
                        m = pe.matmul(PSf[:, z0 + META + 128 * k0:z0 + META + 128 * (k0 + nb)], q,
                                      K[rows, META + 128 * k0:META + 128 * (k0 + nb)], start=True, stop=not last)
                    d = z0 + META + 128 * i
                    pe.matmul(PSf[:, d:d + 128], identb[:, :], maskb[:, :], start=False, stop=True).then_inc(t_z, 1)

                scores(0)
                scores(1)
                for u in range(2 * QB):
                    i, par = u // 2, u % 2
                    pe.wait_ge(t_w, i2 * 32 + (16 * b + u + 1))
                    done = 0
                    gs = tr_groups(i)
                    for j, (k0, nb) in enumerate(gs):
                        pe.wait_ge(t_tc, i2 * (2 * TRG) + (TRG * b + tr_before(u) + j))
                        if j == 0 and u == 0:
                            pe.wait_ge(t_vc, i2 * 6 + (3 * b + 3))
                        for k in range(k0, k0 + nb):
                            n, t0 = (META, 0) if k == 8 else (128, META + 128 * k)
                            m = pe.transpose(PS[0:n, 6, 128 * (k - k0):128 * (k - k0) + 128], wt[par][:, t0:t0 + n], ident[:, :])
                        m.then_inc(t_tr, 1)
                        if j == 0 and u + 2 < 2 * QB:
                            scores(u + 2)
                    if u >= 2 and par == 0:
                        pe.wait_ge(t_ol, i2 * 16 + (8 * b + i))
                    rows = slice(64 * par, 64 * par + 64)
                    for j, (k0, nb) in enumerate(gs):
                        pe.wait_ge(t_tc, i2 * (2 * TRG) + (TRG * b + tr_before(u) + j + 1))
                        for k in range(k0, k0 + nb):
                            n = META if k == 8 else 128
                            m = pe.matmul(PS[rows, 7, 0:128], Vt[0:n, k, rows], wT[par][0:n, k, :],
                                          start=(j == 0 and k == k0), stop=(j == len(gs) - 1 and k == k0 + nb - 1))
                    m.then_inc(t_o, 1)

            with pe.Fori(0, PAIRS // 2) as i2:
                for b in range(2):
                    attention_pair(i2, b)
            pe.wait_ge(t_ol, QB * PAIRS)
            dense(P_O, None)
            norm("f1")
            ffn(P_F1, 1, "f1")
            norm("fin")
            for t in range(QB):
                if t == 0:
                    pe.wait_ge(d_add, 24 * FG + 16 * FG)
                pe.wait_ge(xn_r, XL0["fin"] + t // 2 + 1)
                if t >= 2:
                    pe.wait_ge(o_cpa, t - 1)
                    pe.wait_ge(o_cpv, t - 1)
                for half in range(2):
                    for k in range(4):
                        m = pe.transpose(PS[:, 4 + 2 * (t % 2) + half, 128 * k:128 * k + 128],
                                         hT[:, 4 * half + k, META + 128 * t:META + 128 * t + 128], ident[:, :])
                    m.then_inc(o_tr, 1)


_INS = ["x", "meta_tokens", "gdn_norm_g", "gdn_w_in", "gdn_conv_w", "gdn_a_log", "gdn_dt_bias", "gdn_onorm_g",
        "gdn_w_out", "kv_norm_g", "w_kv", "sb_norm_g", "sb_w_q", "sb_w_o", "ffn_norm_g", "ffn_w_gate_up",
        "ffn_w_down", "final_norm_g"]


def kernel(**inputs):
    import numpy as _np
    import concourse.bacc as _bacc
    from concourse import mybir as _mybir
    from concourse.bass_utils import run_bass_kernel_spmd as _run

    nc = _bacc.Bacc("TRN2", target_bir_lowering=False, num_devices=1)
    arrays, args = {}, []
    for name in _INS:
        a = _np.ascontiguousarray(inputs[name])
        arrays[f"in_{name}"] = a
        args.append(nc.dram_tensor(f"in_{name}", a.shape, _mybir.dt.from_np(a.dtype), kind="ExternalInput").ap())
    out = nc.dram_tensor("out_0", (1, SEQ, D), _mybir.dt.float32, kind="ExternalOutput").ap()
    trunk(nc, *args, out)
    r = _run(nc, [arrays], core_ids=[0])
    return r.results[0]["out_0"]
```

```python
import concourse.bass as bass
from concourse import mybir
from contextlib import ExitStack

F32 = mybir.dt.float32
F32R = mybir.dt.float32r
BF16 = mybir.dt.bfloat16
ALU = mybir.AluOpType
ACT = mybir.ActivationFunctionType

D = 1024
KT = D // 128
SEQ = 1024
META = 16
L = SEQ + META
GH, GD = 8, 128
FF = 2816
EPS = 1e-6
C = 104
NC = L // C
HG = 4
GW = HG * C
LEVELS = 7
LTB = 3
NEG = -1e30
QB = SEQ // 128
PAIRS = 8
ALL_CH = [(0, 348), (348, 346), (694, 346)]
SEQ_CH = [(META, 512), (META + 512, 512)]
SEQ_NCH = [(META + 256 * i, 256) for i in range(4)]
FG = FF // 256


class Phase:

    def __init__(self, jobs, ring, chunks, prev, mm_jobs=None):
        self.jobs, self.ring, self.chunks, self.nch = jobs, ring, chunks, len(chunks)
        self.job0 = prev.job0 + prev.jobs if prev else 0
        self.mm0 = prev.mm0 + prev.mm if prev else 0
        self.mm = (jobs if mm_jobs is None else mm_jobs) * self.nch
        self.slot0 = [prev.slot0[s] + prev.used(s) for s in range(6)] if prev else [0] * 6

    def used(self, s):
        return len(range(s, self.jobs, self.ring)) if s < self.ring else 0


P_IN = Phase(32, 4, ALL_CH, None)
P_GO = Phase(8, 4, ALL_CH, P_IN)
P_F0 = Phase(6 * FG, 6, ALL_CH, P_GO, 4 * FG)
P_KV = Phase(16, 4, ALL_CH, P_F0)
P_Q = Phase(8, 4, SEQ_CH, P_KV)
P_O = Phase(8, 4, SEQ_CH, P_Q)
P_F1 = Phase(6 * FG, 6, SEQ_CH, P_O, 4 * FG)

TAKEN0 = {P_IN: 0, P_GO: 96, P_KV: 120, P_Q: 168, P_O: 184}
SMALL = 16


def level_blocks(b):
    full = C // (2 * b)
    rest = C - full * 2 * b
    return ([(0, full, 2 * b)] if full else []) + ([(full * 2 * b, 1, rest)] if rest else [])


CONSTS = 5 + sum(3 if w > 1 << v else 1 for v in range(LEVELS) for _, _, w in level_blocks(1 << v))


def pair_groups():
    gs = [("V", 0, 0, 4, "act"), ("V", 0, 4, 4, "act"), ("V", 0, 8, 1, "act")]
    for u in range(2 * QB):
        i = u % QB
        gs.append(("W", u, 0, min(4, i + 1), "act"))
        if i > 3:
            gs.append(("W", u, 4, i - 3, "dve"))
        gs.append(("W", u, 8, 1, "dve"))
    return gs + [("O", 0, 0, 3, "act"), ("O", 0, 3, 3, "act"), ("O", 0, 6, 2, "act")]


GROUPS = pair_groups()
NGR = len(GROUPS)
assert NGR % 2 == 0


def copied(n, engine):
    return sum(g[4] == engine for g in GROUPS[:n])


Z0 = (3 * 512, 0)


def group_numbers(kind, u=0):
    return [n for n, g in enumerate(GROUPS) if g[0] == kind and g[1] == u]


def down_banks(nch):
    return list(range(2 * nch, 8)) + list(range(nch, 2 * nch))


def trunk(nc, x, meta_tokens, gdn_norm_g, gdn_w_in, gdn_conv_w, gdn_a_log, gdn_dt_bias, gdn_onorm_g,
          gdn_w_out, kv_norm_g, w_kv, sb_norm_g, sb_w_q, sb_w_o, ffn_norm_g, ffn_w_gate_up,
          ffn_w_down, final_norm_g, out):
    ds = bass.ds
    s_in = nc.dram_tensor("s_in", (NC, 128, 32 * C), F32).ap()
    s_kv = nc.dram_tensor("s_kv", (16, 128, L), F32).ap()
    s_q = nc.dram_tensor("s_q", (8, 128, SEQ), F32).ap()
    s_in_w = s_in.rearrange("c p (t j) -> t p c j", t=32)
    w_in = gdn_w_in[0].rearrange("(k p) n -> p k n", p=128)
    w_go = gdn_w_out[0].rearrange("(k p) n -> p k n", p=128)
    w_kvv = w_kv.rearrange("(k p) n -> p k n", p=128)
    w_q = sb_w_q[0].rearrange("(k p) n -> p k n", p=128)
    w_o = sb_w_o[0].rearrange("(k p) n -> p k n", p=128)
    w_gu = [ffn_w_gate_up[i].rearrange("(k p) n -> p k n", p=128) for i in range(2)]
    w_dn = [ffn_w_down[i].rearrange("(t p) n -> t p n", p=128) for i in range(2)]

    ctx = ExitStack()
    with ctx:
        def sem(name):
            return ctx.enter_context(nc.semaphore(name))

        def keep(name, shape, dt=F32):
            return ctx.enter_context(nc.sbuf_tensor(name, shape, dt))

        hT = keep("hT", [128, KT, L])
        XH = keep("XH", [128, KT, L], F32R)
        XL = keep("XL", [128, KT, L], F32R)
        ident = keep("ident", [128, 128])
        ones = keep("ones", [128, 128])
        tri = keep("tri", [C, C])
        negm = keep("negm", [C, C])
        lvl = keep("lvl", [C, LEVELS, C])
        identb = keep("identb", [128, 128], BF16)
        maskb = keep("maskb", [128, 128], BF16)
        pvec = keep("pvec", [128, 121 + 24])
        epsc = keep("epsc", [128, 4])
        ab = keep("ab", [C, NC, 16])
        sm = keep("sm", [C, NC, 40])
        wab = keep("wab", [128, KT, 16])
        wabH = keep("wabH", [128, KT, 16], F32R)
        wabL = keep("wabL", [128, KT, 16], F32R)
        CONV, GN, ON, KVN, SBN, FN, FIN = 0, 96, 104, 105, 113, 121, 137

        with ExitStack() as a:
            def dense(name, shape, dt=F32):
                return a.enter_context(nc.sbuf_tensor(name, shape, dt))
            raw = [dense(f"raw{s}", [128, D]) for s in range(6)]
            WH = [dense(f"WH{s}", [128, D], F32R) for s in range(6)]
            WL = [dense(f"WL{s}", [128, D], F32R) for s in range(6)]
            rs = dense("rs", [128, 2, 348])
            with ExitStack() as b:
                sqb = b.enter_context(nc.sbuf_tensor("sqb", [128, KT, 348], F32))
                xnb = b.enter_context(nc.sbuf_tensor("xnb", [128, KT, 348], F32))
            with ExitStack() as b:
                cin = b.enter_context(nc.sbuf_tensor("cin", [128, L + 3], F32))
                cac = b.enter_context(nc.sbuf_tensor("cac", [128, L], F32))
                obuf = b.enter_context(nc.sbuf_tensor("obuf", [128, 2, L], F32))
            with ExitStack() as b:
                gact = b.enter_context(nc.sbuf_tensor("gact", [128, L], F32))
                aact = b.enter_context(nc.sbuf_tensor("aact", [128, L], F32))
                AH = b.enter_context(nc.sbuf_tensor("AH", [128, 2, L], F32R))
                AL = b.enter_context(nc.sbuf_tensor("AL", [128, 2, L], F32R))
        with ExitStack() as a:
            prow = a.enter_context(nc.sbuf_tensor("prow", [128, 128], F32))
            prow2 = a.enter_context(nc.sbuf_tensor("prow2", [24, 128], F32))
            xin = a.enter_context(nc.sbuf_tensor("xin", [128, 9, D], F32))
        with ExitStack() as a:
            def core(name, shape, dt=F32):
                return a.enter_context(nc.sbuf_tensor(name, shape, dt))
            Xc = core("Xc", [128, 24, C])
            Gt = core("Gt", [128, 8, C])
            cur = core("cur", [C, 40])
            alog = core("alog", [C, 8])
            dtb = core("dtb", [C, 8])
            t80 = [core(f"t80_{i}", [C, NC, 8]) for i in range(4)]
            B = [{n: core(f"{n}{g}", s) for n, s in [
                ("sq", [128, 2, GW]), ("rr", [128, 2, GW]), ("EG", [128, GW]),
                ("KQ", [128, 2, GW]), ("dec", [128, GW]), ("Qd", [128, GW]), ("NT", [C, GW]),
                ("attn", [C, GW]), ("LT", [C, LTB, GW]), ("U", [C, GW]), ("T", [C, GW]),
                ("X", [C, GW]), ("V", [C, 512]), ("K", [C, 512]), ("Kd", [C, 512]),
                ("Ke", [C, 512]), ("u", [C, 512]), ("S", [128, 512]),
                ("o", [128, GW]), ("kdx", [C, HG])]} for g in range(2)]
            for b in B:
                b["tg"], b["WT"], b["on"] = b["X"], b["dec"], b["Qd"]
        with ExitStack() as a:
            def att(name, shape, dt=F32):
                return a.enter_context(nc.sbuf_tensor(name, shape, dt))
            kraw = [att(f"kraw{i}", [128, L]) for i in range(2)]
            qraw = [att(f"qraw{i}", [128, SEQ]) for i in range(2)]
            KH = [att(f"KH{i}", [128, L], F32R) for i in range(2)]
            KL = [att(f"KL{i}", [128, L], F32R) for i in range(2)]
            QS = [att(f"QS{i}", [128, SEQ], F32R) for i in range(2)]
            vT = att("vT", [128, L])
            Vt = att("Vt", [128, 9, 128])
            kp = [att(f"kp{i}", [128, L]) for i in range(2)]
            sg = [att(f"sg{i}", [128, L]) for i in range(2)]
            Pr = [att(f"Pr{i}", [128, L + 1]) for i in range(2)]
            wt = [att(f"wt{i}", [128, L]) for i in range(2)]
            wT = [att(f"wT{i}", [128, 9, 128]) for i in range(2)]
            ot = att("ot", [128, QB, 128])
            oT = att("oT", [128, SEQ])
        with ExitStack() as a:
            fo = a.enter_context(nc.sbuf_tensor("fo", [128, 2, D], F32))
        PS = ctx.enter_context(nc.psum_tensor("PS", [128, 8, 512], F32))

        raw_in = [sem(f"raw_in{s}") for s in range(6)]
        w_hi = sem("w_hi")
        w_lo = sem("w_lo")
        mm_chunk = sem("mm_chunk")
        taken = sem("taken")
        d_mm = sem("d_mm")
        d_add = sem("d_add")
        sq_r, ss_r, r_r, xn_r, xh_r, xl_r = (sem(n) for n in (
            "sq_r", "ss_r", "r_r", "xn_r", "xh_r", "xl_r"))
        ssln, cin0, c_dt = sem("ssln"), sem("cin0"), sem("c_dt")
        x_in, p_in, cst, cst2, x_tr, x_cpa, x_cpv, p_tr, p_cp = (sem(n) for n in (
            "x_in", "p_in", "cst", "cst2", "x_tr", "x_cpa", "x_cpv", "p_tr", "p_cp"))
        ab_in, ab_h, ab_l, ab_mm, ab_cp, sml = (sem(n) for n in (
            "ab_in", "ab_h", "ab_l", "ab_mm", "ab_cp", "sml"))
        conv = sem("conv")
        ob = sem("ob")
        stored = [sem("stored0"), sem("stored1")]
        silu_g, act_a, act_h, act_l = (sem(n) for n in ("silu_g", "act_a", "act_h", "act_l"))
        o_tr, o_cpa, o_cpv, o_out = sem("o_tr"), sem("o_cpa"), sem("o_cpv"), [sem("o_out0"), sem("o_out1")]

        block = ctx.enter_context(nc.Block())

        NORMS, n0 = {}, 0
        for name, chs, col in (("gdn", ALL_CH, GN), ("f0", ALL_CH, FN), ("kv", ALL_CH, KVN),
                               ("sb", SEQ_NCH, SBN), ("f1", SEQ_NCH, FN + 8), ("fin", SEQ_NCH, FIN)):
            NORMS[name] = (chs, n0, col)
            n0 += len(chs)
        XL0 = {n: NORMS[n][1] for n in NORMS}

        def xn_needed(norm, ph, ch):
            return XL0[norm] + (ch + 1) * (len(NORMS[norm][0]) // ph.nch)

        cs = {}
        for n in ("sq tg ss gb rn eg kn dm qd dmm dec kk tr att nt0 kt kde nt lt u1 t1p t1 x xc tu u "
                  "wt wtc up us op sp sm2 snew oc osq oss orn on1 on2 oh ol").split():
            cs[n] = [sem(f"c_{n}{g}") for g in range(2)]
        c_load, c_gate, c_cur, c_s0 = sem("c_load"), sem("c_gate"), sem("c_cur"), sem("c_s0")
        t_load = [sem("t_load0"), sem("t_load1")]
        (t_vload, t_hi, t_lo, t_z, t_kp, t_sg, t_p, t_w, t_tr, t_ca, t_cd, t_pv, t_o, t_oh, t_ol, t_one) = (
            sem(f"t_{n}") for n in "vload hi lo z kp sg p w tr ca cd pv o oh ol one".split())

        def free(eng, s, n):
            eng.wait_ge(s, n + 1)

        def weights_of(ph, j):
            w = {P_GO: w_go, P_KV: w_kvv, P_Q: w_q, P_O: w_o}[ph]
            return w[:, :, ds(j * 128, 128)]

        def slot3(t):
            return t[:, :].rearrange("p (k n) -> p k n", k=KT)

        def ffn_jobs(layer, g, last=False):
            gu, dn = w_gu[layer], w_dn[layer]
            col = g * 256
            return [gu[:, :, ds(FF + col, 128)], gu[:, :, ds(col + 128, 128)],
                    gu[:, :, ds(FF + col + 128, 128)],
                    None if last else gu[:, :, ds(col + 256, 128)], (dn, g * 2), (dn, g * 2 + 1)]

        @block.sync
        def _(sp):
            sp.dma_start(prow[0:96, :], gdn_conv_w[0].rearrange("w (t p) -> (w t) p", p=128)).then_inc(p_in, 16)
            for col, v in ((GN, gdn_norm_g[0]), (KVN, kv_norm_g), (SBN, sb_norm_g[0])):
                sp.dma_start(prow[col:col + 8, :], v.rearrange("(t p) -> t p", p=128)).then_inc(p_in, 16)
            sp.dma_start(prow[ON:ON + 1, :], gdn_onorm_g).then_inc(p_in, 16)
            sp.dma_start(prow2[0:16, :], ffn_norm_g.rearrange("l (t p) -> (l t) p", p=128)).then_inc(p_in, 16)
            sp.dma_start(prow2[16:24, :], final_norm_g.rearrange("(t p) -> t p", p=128)).then_inc(p_in, 16)
            sp.dma_start(xin[0:META, 8, :], meta_tokens).then_inc(x_in, 16)
            sp.dma_start(xin[:, 0:8, :], x[0].rearrange("(t p) n -> p t n", p=128)).then_inc(x_in, 16)
            sp.dma_start(wab[:, :, :], w_in[:, :, 4 * D:4 * D + 16]).then_inc(ab_in, 16)
            sp.wait_ge(x_cpa, 9)
            sp.wait_ge(x_cpv, 9)
            sp.wait_ge(p_cp, 2)
            for s in range(4):
                sp.dma_start(slot3(raw[s]), w_in[:, :, s * D:s * D + 128]).then_inc(raw_in[s], 16)
            with sp.Fori(0, GH - 1) as h:
                for s in range(4):
                    sp.wait_ge(w_lo, h * 4 + s + 1)
                    sp.dma_start(slot3(raw[s]), w_in[:, :, ds(h * 128 + s * D + 128, 128)]).then_inc(raw_in[s], 16)
            for b in range(2):
                sp.wait_ge(stored[b], 16 * 16)
            sp.wait_ge(mm_chunk, P_GO.mm0)
            sp.dma_start(alog[:, :], gdn_a_log[0:1, :].broadcast_to([C, 8])).then_inc(c_dt, 16)
            sp.dma_start(dtb[:, :], gdn_dt_bias[0:1, :].broadcast_to([C, 8])).then_inc(c_dt, 16)
            with sp.Fori(0, NC) as c:
                for g in range(2):
                    sp.wait_ge(cs["kn"][g], c)
                    sp.wait_ge(cs["sq"][g], c)
                    sp.wait_ge(cs["tr"][g], c)
                sp.dma_start(Xc[:, :, :], s_in[ds(c, 1), :, 0:24 * C].rearrange("a p (t j) -> p (a t) j", j=C)).then_inc(c_load, 16)
                for g in range(2):
                    sp.wait_ge(cs["on2"][g], c)
                sp.dma_start(Gt[:, :, :], s_in[ds(c, 1), :, 24 * C:32 * C].rearrange("a p (t j) -> p (a t) j", j=C)).then_inc(c_gate, 16)

            def chunk_memory(l):
                if l == 0:
                    for g in range(2):
                        sp.wait_ge(cs["kn"][g], NC)
                        sp.wait_ge(cs["sq"][g], NC)
                        sp.wait_ge(cs["tr"][g], NC)
                if l == 2:
                    for g in range(2):
                        sp.wait_ge(cs["on2"][g], NC)
                if l == 3:
                    for g in range(2):
                        sp.wait_ge(cs["ol"][g], NC)
                        sp.wait_ge(cs["snew"][g], NC)

            def plain(ph, before=None):
                for l in range(ph.jobs):
                    if before:
                        before(l)
                    if l < ph.ring:
                        sp.wait_ge(w_lo, ph.job0)
                    else:
                        sp.wait_ge(w_lo, ph.job0 + l - ph.ring + 1)
                    sp.dma_start(slot3(raw[l % 4]), weights_of(ph, l)).then_inc(raw_in[l % 4], 16)

            def ffn(ph, layer):
                sp.wait_ge(w_lo, ph.job0)
                sp.dma_start(slot3(raw[0]), w_gu[layer][:, :, 0:128]).then_inc(raw_in[0], 16)

                def group(g, first, last):
                    for i, src in enumerate(ffn_jobs(layer, g, last)):
                        if src is None:
                            continue
                        s = (1 + i - (last and i > 3)) % 6
                        if not (first and s):
                            sp.wait_ge(w_lo, g * 6 + (ph.job0 + 1 + i - (last and i > 3) - 5))
                        dst = raw[s]
                        if isinstance(src, tuple):
                            sp.dma_start(dst[:, :], src[0][ds(src[1], 1)].rearrange("a p n -> p (a n)")).then_inc(raw_in[s], 16)
                        else:
                            sp.dma_start(slot3(dst), src).then_inc(raw_in[s], 16)
                group(0, True, False)
                with sp.Fori(1, FG - 1) as g:
                    group(g, False, False)
                group(FG - 1, False, True)

            plain(P_GO, chunk_memory)
            ffn(P_F0, 0)
            plain(P_KV)
            plain(P_Q)
            sp.wait_ge(mm_chunk, P_O.mm0)
            for b in range(2):
                sp.wait_ge(stored[b], 16 * 28)

            def load_head(j, b):
                for half in range(2):
                    rows = slice(64 * half, 64 * half + 64)
                    sp.dma_start(kraw[b][rows, :], s_kv[ds(j, 1), 64 * b:64 * b + 64].rearrange("a p n -> p (a n)")).then_inc(t_load[b], 16)
                    sp.dma_start(qraw[b][rows, :], s_q[ds(j, 1), 64 * b:64 * b + 64].rearrange("a p n -> p (a n)")).then_inc(t_load[b], 16)

            def load_v(j):
                sp.dma_start(vT[:, :], s_kv[ds(j + 8, 1)].rearrange("a p n -> p (a n)")).then_inc(t_vload, 16)
            load_head(0, 0)
            load_v(0)
            load_head(0, 1)
            with sp.Fori(0, PAIRS - 1) as i:
                sp.wait_ge(t_lo, i * 4 + 2)
                load_head(i + 1, 0)
                sp.wait_ge(t_tr, i * NGR + 3)
                load_v(i + 1)
                sp.wait_ge(t_lo, i * 4 + 4)
                load_head(i + 1, 1)
            sp.wait_ge(t_lo, PAIRS * 4)
            plain(P_O)
            ffn(P_F1, 1)
            for t in range(QB):
                sp.wait_ge(o_cpa, t + 1)
                sp.wait_ge(o_cpv, t + 1)
                sp.dma_start(out[0, t * 128:(t + 1) * 128, :], fo[:, t % 2, :]).then_inc(o_out[t % 2], 16)
            for b in range(2):
                sp.wait_ge(o_out[b], 16 * QB // 2)
            for b in range(2):
                sp.wait_ge(stored[b], 16 * 28)

        @block.gpsimd
        def _(pool):
            pool.memset(ones[:, :], 1.0).then_inc(cst, 1)
            pool.memset(ident[:, :], 0.0).then_inc(cst, 1)
            pool.memset(negm[:, :], 0.0).then_inc(cst, 1)
            pool.memset(tri[:, :], 1.0).then_inc(cst, 1)
            pool.memset(lvl[:, :, :], 1.0).then_inc(cst, 1)
            pool.memset(maskb[:, :], NEG).then_inc(cst, 1)
            pool.memset(identb[:, :], 0.0).then_inc(cst, 1)
            pool.memset(epsc[:, 0:1], EPS).then_inc(cst, 1)
            pool.memset(epsc[:, 1:2], 1.0).then_inc(cst, 1)
            pool.wait_ge(cst, 9)
            pool.affine_select(out=ident[:, :], in_=ident[:, :], compare_op=ALU.not_equal, fill=1.0, base=0,
                               pattern=[[-1, 128]], channel_multiplier=1).then_inc(cst2, 1)
            pool.affine_select(out=identb[:, :], in_=identb[:, :], compare_op=ALU.not_equal, fill=1.0, base=0,
                               pattern=[[-1, 128]], channel_multiplier=1).then_inc(cst2, 1)
            pool.affine_select(out=tri[:, :], in_=tri[:, :], compare_op=ALU.is_ge, fill=0.0, base=0,
                               pattern=[[1, C]], channel_multiplier=-1).then_inc(cst2, 1)
            pool.affine_select(out=negm[:, :], in_=negm[:, :], compare_op=ALU.is_ge, fill=NEG, base=0,
                               pattern=[[1, C]], channel_multiplier=-1).then_inc(cst2, 1)
            pool.affine_select(out=maskb[:, :], in_=maskb[:, :], compare_op=ALU.is_ge, fill=0.0, base=0,
                               pattern=[[1, 128]], channel_multiplier=-1).then_inc(cst2, 1)
            n = 5
            for v in range(LEVELS):
                b = 1 << v
                for col0, cnt, w in level_blocks(b):
                    if w <= b:
                        pool.memset(lvl[:, v, col0:C], 0.0).then_inc(cst2, 1)
                        n += 1
                        continue
                    view = lvl[:, v, col0:col0 + cnt * w].rearrange("p (m w) -> p m w", w=w)
                    pool.affine_select(out=view, in_=view, compare_op=ALU.is_ge, fill=0.0, base=-col0,
                                       pattern=[[-2 * b, cnt], [0, w]], channel_multiplier=1).then_inc(cst2, 1)
                    pool.wait_ge(cst2, n + 1)
                    pool.affine_select(out=view, in_=view, compare_op=ALU.is_ge, fill=0.0, base=col0 + b - 1,
                                       pattern=[[2 * b, cnt], [0, w]], channel_multiplier=-1).then_inc(cst2, 1)
                    pool.wait_ge(cst2, n + 2)
                    pool.memset(view[:, :, 0:b], 0.0).then_inc(cst2, 1)
                    n += 3
            assert n == CONSTS, n
            pool.wait_ge(cst2, n)

            with pool.Fori(0, GH) as h:
                for s in range(4):
                    pool.wait_ge(ob, h * 3 + s + 1) if s < 3 else pool.wait_ge(taken, h * 12 + 12)
                    pool.dma_start(s_in_w[ds(h + s * 8, 1)].rearrange("t p c j -> p (t c) j"),
                                   obuf[:, s % 2, :].rearrange("p (c j) -> p c j", j=C)).then_inc(stored[s % 2], 16)

            pool.wait_ge(mm_chunk, P_GO.mm0)
            for b in range(2):
                pool.wait_ge(stored[b], 16 * 16)
            for g in range(2):
                pool.memset(B[g]["S"][:, :], 0.0).then_inc(c_s0, 1)
            pool.wait_ge(sml, SMALL)
            with pool.Fori(0, NC) as c:
                for g in range(2):
                    pool.wait_ge(cs["us"][g], c)
                    pool.wait_ge(cs["nt0"][g], c)
                    pool.wait_ge(cs["tg"][g], c)
                    pool.wait_ge(cs["nt"][g], c)
                    pool.wait_ge(cs["kde"][g], c * 2)
                pool.tensor_copy(cur[:, :], sm[:, ds(c, 1), :].rearrange("p a n -> p (a n)")).then_inc(c_cur, 1)
                pool.wait_ge(c_load, c * 16 + 16)
                pool.wait_ge(c_cur, c + 1)
                for g in range(2):
                    b, hs = B[g], slice(HG * g, HG * g + HG)
                    pool.wait_ge(cs["ss"][g], c)
                    pool.wait_ge(cs["oss"][g], c)
                    src = Xc[:, 0:16, :].rearrange("p (w h) j -> p w h j", w=2)[:, :, hs, :]
                    pool.tensor_tensor(b["sq"][:, :, :].rearrange("p w (h j) -> p w h j", h=HG), src, src,
                                       ALU.mult).then_inc(cs["sq"][g], 1)
                    pool.wait_ge(cs["gb"][g], c)
                    pool.tensor_tensor(b["tg"][:, :].rearrange("p (h j) -> p h j", h=HG),
                                       tri[:, :].unsqueeze(1).broadcast_to([C, HG, C]),
                                       cur[:, 32 + HG * g:32 + HG * g + HG].unsqueeze(2).broadcast_to([C, HG, C]),
                                       ALU.mult).then_inc(cs["tg"][g], 1)
                for v in range(LEVELS):
                    for g in range(2):
                        b = B[g]
                        if v == 0:
                            pool.wait_ge(cs["nt"][g], c + 1)
                        if v >= LTB:
                            if v == LTB:
                                pool.wait_ge(cs["t1p"][g], c + 1)
                                pool.wait_ge(cs["u1"][g], c + 1)
                            else:
                                pool.wait_ge(cs["x"][g], c * (LEVELS - 1) + (v - LTB))
                        pool.tensor_tensor(b["LT"][:, v % LTB, :].rearrange("p (h j) -> p h j", h=HG),
                                           b["NT"][:, :].rearrange("p (h j) -> p h j", h=HG),
                                           lvl[:, v, :].unsqueeze(1).broadcast_to([C, HG, C]),
                                           ALU.mult).then_inc(cs["lt"][g], 1)
                        if v == 2:
                            k3 = b["K"][:, :].rearrange("p (h d) -> p h d", h=HG)
                            pool.wait_ge(cs["kt"][g], c + 1)
                            pool.wait_ge(cs["dec"][g], c * 2 + 1)
                            pool.tensor_tensor(b["Kd"][:, :].rearrange("p (h d) -> p h d", h=HG), k3,
                                               b["kdx"][:, :].unsqueeze(2).broadcast_to([C, HG, 128]),
                                               ALU.mult).then_inc(cs["kde"][g], 1)
                            pool.tensor_tensor(b["Ke"][:, :].rearrange("p (h d) -> p h d", h=HG), k3,
                                               cur[:, 24 + HG * g:24 + HG * g + HG].unsqueeze(2).broadcast_to([C, HG, 128]),
                                               ALU.mult).then_inc(cs["kde"][g], 1)
                for g in range(2):
                    b = B[g]
                    pool.wait_ge(cs["op"][g], c + 1)
                    s3 = b["S"][:, :].rearrange("p (h d) -> p h d", h=HG)
                    egl = b["EG"][:, :].rearrange("p (h j) -> p h j", h=HG)[:, :, C - 1:C]
                    pool.tensor_tensor(s3, s3, egl.broadcast_to([128, HG, 128]), ALU.mult).then_inc(cs["sm2"][g], 1)
            for g in range(2):
                pool.wait_ge(cs["ol"][g], NC)

            with pool.Fori(0, 4) as i:
                for s in range(4):
                    pool.wait_ge(taken, i * 12 + (TAKEN0[P_KV] + 3 * (s + 1)))
                    pool.dma_start(s_kv[ds(i * 4 + s, 1)].rearrange("a p n -> p (a n)"), obuf[:, s % 2, :]).then_inc(stored[s % 2], 16)
            with pool.Fori(0, 2) as i:
                for s in range(4):
                    pool.wait_ge(taken, i * 8 + (TAKEN0[P_Q] + 2 * (s + 1)))
                    pool.dma_start(s_q[ds(i * 4 + s, 1)].rearrange("a p n -> p (a n)"), obuf[:, s % 2, 0:SEQ]).then_inc(stored[s % 2], 16)
            for b in range(2):
                pool.wait_ge(stored[b], 16 * 28)
            pool.wait_ge(mm_chunk, P_O.mm0)
            for b in range(2):
                pool.memset(Pr[b][:, L:L + 1], 1.0).then_inc(t_one, 1)

            def split_head(j, b):
                pool.wait_ge(t_hi, j * 4 + (2 * b + 2))
                pool.tensor_tensor(KL[b][:, :], kraw[b][:, :], KH[b][:, :].bitcast(F32), ALU.subtract).then_inc(t_lo, 1)
                pool.wait_ge(t_lo, j * 4 + (2 * b + 1))
                pool.tensor_tensor(QS[b][64:128, :], qraw[b][64:128, :], QS[b][64:128, :].bitcast(F32),
                                   ALU.subtract).then_inc(t_lo, 1)
                pool.wait_ge(t_lo, j * 4 + (2 * b + 2))

            def result(j):
                xh, xl = (X[:, ds(j, 1), META:L].rearrange("p a n -> p (a n)") for X in (XH, XL))
                free(pool, t_ca, (j + 1) * copied(NGR, "act"))
                pool.wait_ge(t_one, 2)
                pool.tensor_copy(xh, oT[:, :]).then_inc(t_oh, 1)
                pool.wait_ge(t_oh, j + 1)
                pool.tensor_tensor(xl, oT[:, :], xh.bitcast(F32), ALU.subtract).then_inc(t_ol, 1)

            pool.sem_inc(t_ol, 1)
            split_head(0, 0)
            split_head(0, 1)
            with pool.Fori(0, PAIRS - 1) as i:
                split_head(i + 1, 0)
                split_head(i + 1, 1)
                result(i)
            result(PAIRS - 1)

        @block.scalar
        def _(act):
            def hi(s, count):
                act.wait_ge(raw_in[s], count)
                act.activation(WH[s][:, :], raw[s][:, :], ACT.Copy).then_inc(w_hi, 1)

            def norm(name, h_ready, meanwhile=None):
                chs, n0, _ = NORMS[name]

                def square(j):
                    t0, n = chs[j]
                    h_ready(act, j)
                    act.activation(sqb[:, :, 0:n], hT[:, :, t0:t0 + n], ACT.Square).then_inc(sq_r, 1)

                square(0)
                for j, (t0, n) in enumerate(chs):
                    act.wait_ge(ss_r, n0 + j + 1)
                    if j + 1 < len(chs):
                        square(j + 1)
                    if n0 + j >= 2:
                        act.wait_ge(xn_r, n0 + j - 1)
                    r = rs[:, (n0 + j) % 2, 0:n]
                    act.activation(r, PS[:, j, 0:n], ACT.Ln, bias=epsc[:, 0:1], scale=1.0 / D).then_inc(ssln, 1)
                    act.wait_ge(ssln, n0 + j + 1)
                    act.activation(r, r, ACT.Exp, scale=-0.5).then_inc(r_r, 1)
                    act.wait_ge(xn_r, n0 + j + 1)
                    if name != "fin":
                        act.activation(XH[:, :, t0:t0 + n], xnb[:, :, 0:n], ACT.Copy).then_inc(xh_r, 1)
                    if meanwhile and j == 1:
                        meanwhile()

            for t in range(9):
                n = META if t == 8 else 128
                t0 = 0 if t == 8 else META + 128 * t
                act.wait_ge(x_tr, 2 * t + 1)
                act.activation(hT[:, 0:4, t0:t0 + n],
                               PS[:, 2 * (t % 3), :].rearrange("p (k n) -> p k n", k=4)[:, :, 0:n], ACT.Copy).then_inc(x_cpa, 1)
            act.wait_ge(x_cpa, 9)

            def first_his():
                act.wait_ge(ab_in, 16)
                act.activation(wabH[:, :, :], wab[:, :, :], ACT.Copy).then_inc(ab_h, 1)
                for s in range(4):
                    hi(s, 16)
            norm("gdn", lambda e, j: e.wait_ge(x_cpv, 9), first_his)
            act.wait_ge(xl_r, 3)

            def in_job(h, s, last):
                b = s % 2
                for ch, (t0, n) in enumerate(ALL_CH):
                    act.wait_ge(mm_chunk, h * 12 + (3 * s + ch + 1))
                    src = PS[:, 3 * b + ch, 0:n]
                    if s < 3:
                        act.activation(cin[:, 3 + t0:3 + t0 + n], src, ACT.Copy).then_inc(taken, 1)
                    else:
                        if ch == 0:
                            act.wait_ge(stored[1], h * 32 + 16)
                        act.activation(obuf[:, 1, t0:t0 + n], src, ACT.Silu).then_inc(taken, 1)
                if not last:
                    hi(s, h * 16 + 32)
                if s < 3:
                    act.wait_ge(conv, h * 12 + 4 * (s + 1))
                    act.wait_ge(stored[b], h * 32 + 16 * (s // 2))
                    act.activation(obuf[:, b, :], cac[:, :], ACT.Silu).then_inc(ob, 1)

            with act.Fori(0, GH - 1) as h:
                for s in range(4):
                    in_job(h, s, False)
            for s in range(4):
                in_job(GH - 1, s, True)

            act.wait_ge(c_dt, 32)
            act.wait_ge(sml, 2)
            act.activation(t80[1][:, :, :], t80[1][:, :, :], ACT.Exp, scale=-1.0).then_inc(sml, 1)
            act.activation(t80[2][:, :, :], ab[:, :, 8:16], ACT.Exp, scale=-1.0).then_inc(sml, 1)
            act.activation(alog[:, :], alog[:, :], ACT.Exp).then_inc(sml, 1)
            act.wait_ge(sml, 5)
            act.activation(t80[1][:, :, :], t80[1][:, :, :], ACT.Ln, bias=epsc[0:C, 1:2]).then_inc(sml, 1)
            act.wait_ge(sml, 13)
            act.activation(sm[:, :, 0:8], PS[0:C, 7, 0:8 * NC].rearrange("p (c h) -> p c h", h=8), ACT.Copy).then_inc(sml, 1)
            act.wait_ge(sml, 14)
            act.activation(t80[3][:, :, :], sm[:, :, 0:8], ACT.Exp).then_inc(sml, 1)
            with act.Fori(0, NC) as c:
                for g in range(2):
                    b = B[g]
                    act.wait_ge(cs["ss"][g], c + 1)
                    act.wait_ge(cs["on1"][g], c)
                    act.activation(b["rr"][:, :, :], PS[:, 4 * g:4 * g + 2, 0:GW], ACT.Ln, bias=epsc[:, 0:1]).then_inc(cs["rn"][g], 1)
                    act.wait_ge(cs["rn"][g], c * 2 + 1)
                    act.activation(b["rr"][:, :, :], b["rr"][:, :, :], ACT.Exp, scale=-0.5).then_inc(cs["rn"][g], 1)
                    act.wait_ge(cs["gb"][g], c + 1)
                    act.wait_ge(cs["sm2"][g], c)
                    act.activation(b["EG"][:, :], PS[:, 4 * g + 2, 0:GW], ACT.Exp).then_inc(cs["eg"][g], 1)
                for g in range(2):
                    b = B[g]
                    act.wait_ge(cs["dmm"][g], c + 1)
                    act.activation(b["kdx"][:, :], b["kdx"][:, :], ACT.Exp).then_inc(cs["dec"][g], 1)
                    act.activation(b["dec"][0:C, :], b["dec"][0:C, :], ACT.Exp).then_inc(cs["dec"][g], 1)
                for g in range(2):
                    b = B[g]
                    act.wait_ge(cs["tr"][g], c + 1)
                    act.activation(b["K"][:, :], PS[0:C, 4 * g + 2, :], ACT.Copy)
                    act.activation(b["V"][:, :], PS[0:C, 4 * g + 3, :], ACT.Copy).then_inc(cs["kt"][g], 1)
                for v in range(LEVELS - 1):
                    for g in range(2):
                        b = B[g]
                        act.wait_ge(cs["x"][g], c * (LEVELS - 1) + v + 1)
                        act.activation(b["X"][:, :], PS[0:C, 4 * g + 1, 0:GW], ACT.Copy).then_inc(cs["xc"][g], 1)
                for g in range(2):
                    b = B[g]
                    act.wait_ge(cs["wt"][g], c + 1)
                    act.activation(b["WT"][:, :], PS[:, 4 * g, 0:GW], ACT.Copy).then_inc(cs["wtc"][g], 1)
                for g in range(2):
                    b = B[g]
                    act.wait_ge(cs["op"][g], c + 1)
                    act.activation(b["sq"][:, 0, :], PS[:, 4 * g + 2, 0:GW], ACT.Square).then_inc(cs["osq"][g], 1)
                    act.activation(b["o"][:, :], PS[:, 4 * g + 2, 0:GW], ACT.Copy).then_inc(cs["oc"][g], 1)
                for g in range(2):
                    b = B[g]
                    act.wait_ge(cs["oss"][g], c + 1)
                    act.activation(b["rr"][:, 0, :], PS[:, 4 * g, 0:GW], ACT.Ln, bias=epsc[:, 0:1], scale=1.0 / GD).then_inc(cs["orn"][g], 1)
                    act.wait_ge(cs["orn"][g], c * 2 + 1)
                    act.activation(b["rr"][:, 0, :], b["rr"][:, 0, :], ACT.Exp, scale=-0.5).then_inc(cs["orn"][g], 1)
                for g in range(2):
                    b = B[g]
                    act.wait_ge(cs["on2"][g], c + 1)
                    act.activation(XH[:, HG * g:HG * g + HG, ds(c * C, C)],
                                   b["on"][:, :].rearrange("p (h j) -> p h j", h=HG), ACT.Copy).then_inc(cs["oh"][g], 1)
            for g in range(2):
                act.wait_ge(cs["ol"][g], NC)

            def first_splits(ph):
                act.wait_ge(mm_chunk, ph.mm0)
                for s in range(4):
                    hi(s, 16 * (ph.slot0[s] + 1))

            def next_split(ph, l):
                if l + 4 < ph.jobs:
                    act.wait_ge(mm_chunk, ph.mm0 + ph.nch * (l + 1))
                    hi(l % 4, 16 * (ph.slot0[l % 4] + l // 4 + 2))

            def ffn(ph, layer, name, h_ready):
                nch, chs = ph.nch, ph.chunks
                t00 = chs[0][0]
                W = chs[-1][0] + chs[-1][1] - t00
                DU = 8 * nch
                d0 = 24 * FG * layer
                a0 = 6 * FG * layer

                def activate(g, t):
                    for ch, (t0, n) in enumerate(chs):
                        act.wait_ge(mm_chunk, g * (4 * nch) + (ph.mm0 + 2 * nch * t + ch + 1))
                        if ch == 0:
                            act.wait_ge(act_a, g * (2 * nch) + (a0 + nch * t))
                        act.activation(gact[:, t0 - t00:t0 - t00 + n], PS[:, ch, 0:n], ACT.Silu).then_inc(silu_g, 1)
                    act.wait_ge(act_a, g * (2 * nch) + (a0 + nch * (t + 1)))
                    act.wait_ge(d_mm, g * DU + d0)
                    act.activation(AH[:, t, 0:W], aact[:, 0:W], ACT.Copy).then_inc(act_h, 1)

                def body(g, nxt):
                    activate(g, 0)
                    activate(g, 1)
                    if nxt:
                        for s in (1, 2, 3, 4):
                            act.wait_ge(mm_chunk, g * (4 * nch) + (ph.mm0 + nch * (s + 1)))
                            hi(s, g * 16 + 16 * (ph.slot0[s] + 2))
                        act.wait_ge(d_mm, g * DU + (d0 + DU))
                        hi(5, g * 16 + 16 * (ph.slot0[5] + 2))
                    if nxt == 1:
                        hi(0, g * 16 + 16 * (ph.slot0[0] + 3))

                act.wait_ge(mm_chunk, ph.mm0)
                hi(0, 16 * (ph.slot0[0] + 1))
                norm(name, h_ready)
                for s in range(1, 6):
                    hi(s, 16 * (ph.slot0[s] + 1))
                act.wait_ge(mm_chunk, ph.mm0 + nch)
                hi(0, 16 * (ph.slot0[0] + 2))
                act.wait_ge(xl_r, XL0[name] + len(NORMS[name][0]))
                with act.Fori(0, FG - 2) as g:
                    body(g, 1)
                body(FG - 2, 2)
                body(FG - 1, 0)

            first_splits(P_GO)
            for l in range(P_GO.jobs):
                next_split(P_GO, l)
            ffn(P_F0, 0, "f0", lambda e, j: e.wait_ge(taken, TAKEN0[P_GO] + P_GO.mm - 2 + j))

            def project(ph, name, tiles0):
                act.wait_ge(xl_r, XL0[name] + len(NORMS[name][0]))
                for l in range(ph.jobs):
                    b = l % 2
                    act.wait_ge(stored[b], 16 * ((tiles0 + l) // 2))
                    for ch, (t0, n) in enumerate(ph.chunks):
                        o0 = t0 - ph.chunks[0][0]
                        act.wait_ge(mm_chunk, ph.mm0 + ph.nch * l + ch + 1)
                        act.activation(obuf[:, b, o0:o0 + n], PS[:, ph.nch * b + ch, 0:n], ACT.Copy).then_inc(taken, 1)
                    next_split(ph, l)

            first_splits(P_KV)
            act.wait_ge(d_mm, 24 * FG)
            norm("kv", lambda e, j: e.wait_ge(d_add, 24 * (FG - 1) + 8 * (j + 1)))
            project(P_KV, "kv", 32)
            first_splits(P_Q)
            for b in range(2):
                act.wait_ge(stored[b], 16 * 24)
            norm("sb", lambda e, j: None)
            project(P_Q, "sb", 48)

            PSf = PS[:, :, :].rearrange("p b n -> p (b n)")

            def sigmoids(j, u):
                i, b = u % QB, u % 2
                n = META + 128 * (i + 1)
                z = PSf[:, Z0[b]:Z0[b] + n]
                act.wait_ge(t_z, j * 16 + (u + 1))
                free(act, t_p, j * 16 + max(u - 1, 0))
                act.activation(kp[b][:, 0:n], z, ACT.Sigmoid, scale=-0.125).then_inc(t_kp, 1)
                free(act, t_w, j * 16 + max(u - 1, 0))
                act.activation(sg[b][:, 0:n], z, ACT.Sigmoid, scale=0.125).then_inc(t_sg, 1)

            def copy_group(j, n):
                kind, u, k0, nb, _ = GROUPS[n]
                src = PS[:, 5 + n % 2, 0:128 * nb].rearrange("p (k n) -> p k n", n=128)
                rows = META if k0 == 8 else 128
                act.wait_ge(t_tr, j * NGR + (n + 1))
                if kind == "O":
                    free(act, t_ol, j)
                    act.activation(oT[:, 128 * k0:128 * (k0 + nb)], PS[:, 5 + n % 2, 0:128 * nb], ACT.Copy).then_inc(t_ca, 1)
                    return
                if kind == "W":
                    free(act, t_pv, j * 16 + max(u - 1, 0))
                dst = Vt if kind == "V" else wT[u % 2]
                act.activation(dst[0:rows, k0:k0 + nb, :], src[0:rows], ACT.Copy).then_inc(t_ca, 1)

            def split_head(j, b):
                act.wait_ge(t_load[b], j * 64 + 64)
                act.activation(KH[b][:, :], kraw[b][:, :], ACT.Copy).then_inc(t_hi, 1)
                act.activation(QS[b][:, :], qraw[b][:, :], ACT.Copy).then_inc(t_hi, 1)

            def pair(j, last):
                for n in group_numbers("V"):
                    copy_group(j, n)
                for u in range(2 * QB):
                    if not (last and u == 2 * QB - 1):
                        sigmoids(j, u + 1)
                    for n in group_numbers("W", u):
                        if GROUPS[n][4] == "act":
                            copy_group(j, n)
                    if u == QB:
                        head_out(j, 0)
                    if u == QB + 1 and not last:
                        split_head(j + 1, 0)
                if not last:
                    split_head(j + 1, 1)
                head_out(j, 1)
                for n in group_numbers("O"):
                    copy_group(j, n)

            def head_out(j, b):
                free(act, t_pv, j * 16 + (8 * b + 8))
                act.activation(ot[:, :, 64 * b:64 * b + 64], PS[:, 7, :].rearrange("p (i d) -> p i d", d=64), ACT.Copy).then_inc(t_o, 1)

            act.sem_inc(t_ca, 1)
            split_head(0, 0)
            split_head(0, 1)
            sigmoids(0, 0)
            with act.Fori(0, PAIRS - 1) as j:
                pair(j, False)
            pair(PAIRS - 1, True)
            free(act, t_ol, PAIRS)

            first_splits(P_O)
            for l in range(P_O.jobs):
                next_split(P_O, l)
            ffn(P_F1, 1, "f1", lambda e, j: e.wait_ge(taken, TAKEN0[P_O] + P_O.mm))
            act.wait_ge(d_mm, 24 * FG + 16 * FG)
            norm("fin", lambda e, j: e.wait_ge(d_add, 24 * FG + 16 * (FG - 1) + 8 * (j // 2 + 1)))
            for t in range(QB):
                act.wait_ge(o_tr, 2 * t + 1)
                if t >= 2:
                    act.wait_ge(o_out[t % 2], 16 * (t // 2))
                act.activation(fo[:, t % 2, 0:512], PS[:, 4 + 2 * (t % 2), :], ACT.Copy).then_inc(o_cpa, 1)

        @block.vector
        def _(dve):
            def norm(name, meanwhile=None):
                chs, n0, col = NORMS[name]
                for j, (t0, n) in enumerate(chs):
                    if meanwhile and j == 2:
                        meanwhile()
                    dve.wait_ge(r_r, n0 + j + 1)
                    if name != "fin" and n0 + j:
                        dve.wait_ge(xl_r, n0 + j)
                        dve.wait_ge(xh_r, n0 + j)
                    if name == "fin":
                        for m in range(KT):
                            dst = hT[:, m, t0:t0 + n]
                            x_ = dve.scalar_tensor_tensor(dst, hT[:, m, t0:t0 + n], pvec[:, col + m:col + m + 1],
                                                          rs[:, (n0 + j) % 2, 0:n], ALU.mult, ALU.mult)
                        x_.then_inc(xn_r, 1)
                        continue
                    for m in range(KT):
                        x_ = dve.scalar_tensor_tensor(xnb[:, m, 0:n], hT[:, m, t0:t0 + n], pvec[:, col + m:col + m + 1],
                                                      rs[:, (n0 + j) % 2, 0:n], ALU.mult, ALU.mult)
                    x_.then_inc(xn_r, 1)
                    dve.wait_ge(xh_r, n0 + j + 1)
                    dve.wait_ge(xn_r, n0 + j + 1)
                    dve.tensor_tensor(XL[:, :, t0:t0 + n], xnb[:, :, 0:n], XH[:, :, t0:t0 + n].bitcast(F32),
                                      ALU.subtract).then_inc(xl_r, 1)

            def lo(s, count):
                dve.wait_ge(w_hi, count)
                dve.tensor_tensor(WL[s][:, :], raw[s][:, :], WH[s][:, :].bitcast(F32), ALU.subtract).then_inc(w_lo, 1)

            for t in range(9):
                n = META if t == 8 else 128
                t0 = 0 if t == 8 else META + 128 * t
                dve.wait_ge(x_tr, 2 * t + 2)
                dve.tensor_copy(hT[:, 4:8, t0:t0 + n],
                                PS[:, 2 * (t % 3) + 1, :].rearrange("p (k n) -> p k n", k=4)[:, :, 0:n]).then_inc(x_cpv, 1)
            dve.wait_ge(p_tr, 2)
            dve.tensor_copy(pvec[:, 0:121], PS[:, 6, 0:121]).then_inc(p_cp, 1)
            dve.tensor_copy(pvec[:, 121:145], PS[:, 7, 0:24]).then_inc(p_cp, 1)
            dve.wait_ge(p_cp, 2)

            def first_los():
                dve.wait_ge(ab_h, 1)
                dve.tensor_tensor(wabL[:, :, :], wab[:, :, :], wabH[:, :, :].bitcast(F32), ALU.subtract).then_inc(ab_l, 1)
                for s in range(4):
                    lo(s, s + 1)
            norm("gdn", first_los)
            dve.wait_ge(xh_r, 3)
            dve.wait_ge(xl_r, 3)
            dve.memset(cin[:, 0:3], 0.0).then_inc(cin0, 1)
            for ch, (t0, n) in enumerate(ALL_CH):
                dve.wait_ge(ab_mm, ch + 1)
                dve.tensor_copy(cac[0:16, t0:t0 + n], PS[0:16, 3 + ch, 0:n]).then_inc(ab_cp, 1)
            dve.wait_ge(ab_mm, 4)
            dve.tensor_copy(ab[:, :, :], PS[0:C, 6, 0:16 * NC].rearrange("p (c n) -> p c n", n=16)).then_inc(ab_cp, 1)

            def in_job(h, s, last):
                if s < 3:
                    dve.wait_ge(taken, h * 12 + (3 * s + 3))
                    dve.wait_ge(ob, h * 3 + s)
                    dve.wait_ge(cin0, 1)
                    for i in range(4):
                        w = pvec[:, ds(h + (CONV + 24 * i + 8 * s), 1)]
                        dve.wait_ge(conv, h * 12 + (4 * s + i))
                        if i == 0:
                            y = dve.tensor_scalar(cac[:, :], cin[:, 0:L], w, None, ALU.mult)
                        else:
                            y = dve.scalar_tensor_tensor(cac[:, :], cin[:, i:i + L], w, cac[:, :], ALU.mult, ALU.add)
                        y.then_inc(conv, 1)
                if not last:
                    lo(s, h * 4 + (s + 5))
            with dve.Fori(0, GH - 1) as h:
                for s in range(4):
                    in_job(h, s, False)
            for s in range(4):
                in_job(GH - 1, s, True)

            a3, b3 = ab[:, :, 0:8], ab[:, :, 8:16]
            dve.wait_ge(c_dt, 32)
            dve.wait_ge(ab_cp, 4)
            dve.tensor_tensor(t80[0][:, :, :], a3, dtb[:, :].unsqueeze(1).broadcast_to([C, NC, 8]), ALU.add).then_inc(sml, 1)
            dve.wait_ge(sml, 1)
            dve.scalar_tensor_tensor(t80[1][:, :, :], t80[0][:, :, :], -1.0, t80[0][:, :, :], ALU.mult, ALU.max).then_inc(sml, 1)
            dve.wait_ge(sml, 6)
            dve.tensor_scalar(t80[0][:, :, :], t80[0][:, :, :], 0.0, None, ALU.max).then_inc(sml, 1)
            dve.wait_ge(sml, 7)
            dve.tensor_tensor(t80[0][:, :, :], t80[0][:, :, :], t80[1][:, :, :], ALU.add).then_inc(sml, 1)
            dve.tensor_scalar(t80[2][:, :, :], t80[2][:, :, :], 1.0, None, ALU.add).then_inc(sml, 1)
            dve.wait_ge(sml, 9)
            dve.scalar_tensor_tensor(sm[:, :, 32:40], t80[0][:, :, :], -1.0, alog[:, :].unsqueeze(1).broadcast_to([C, NC, 8]),
                                     ALU.mult, ALU.mult).then_inc(sml, 1)
            dve.reciprocal(sm[:, :, 16:24], t80[2][:, :, :]).then_inc(sml, 1)
            dve.wait_ge(sml, 11)
            dve.tensor_scalar(sm[:, :, 8:16], sm[:, :, 16:24], -1.0, None, ALU.mult).then_inc(sml, 1)
            dve.wait_ge(sml, 15)
            dve.tensor_scalar(sm[:, :, 24:32], t80[3][:, :, :], -1.0, None, ALU.mult).then_inc(sml, 1)
            with dve.Fori(0, NC) as c:
                dve.wait_ge(c_cur, c + 1)
                dve.wait_ge(c_load, c * 16 + 16)
                for g in range(2):
                    b = B[g]
                    v3 = lambda t: t.rearrange("p (h j) -> p h j", h=HG)
                    q3 = Xc[:, HG * g:HG * g + HG, :].rearrange("p h j -> p (h j)")
                    k3 = Xc[:, 8 + HG * g:8 + HG * g + HG, :].rearrange("p h j -> p (h j)")
                    dve.wait_ge(cs["eg"][g], c + 1)
                    gj = cur[:, HG * g:HG * g + HG].unsqueeze(2)
                    gb = v3(PS[0:C, 4 * g + 2, 0:GW])
                    dve.tensor_tensor(v3(b["dec"][0:C, :]), gb, gj.broadcast_to([C, HG, C]), ALU.subtract)
                    dve.tensor_tensor(b["kdx"][:, :].unsqueeze(2), gb[:, :, C - 1:C], gj, ALU.subtract).then_inc(cs["dm"][g], 1)
                    dve.wait_ge(cs["dm"][g], c + 1)
                    dve.tensor_tensor(v3(b["dec"][0:C, :]), v3(b["dec"][0:C, :]), negm[:, :].unsqueeze(1).broadcast_to([C, HG, C]),
                                      ALU.add).then_inc(cs["dmm"][g], 1)
                    dve.wait_ge(cs["rn"][g], c * 2 + 2)
                    dve.tensor_tensor(b["KQ"][:, 0, :], k3, b["rr"][:, 1, :], ALU.mult)
                    dve.scalar_tensor_tensor(b["KQ"][:, 1, :], q3, GD ** -0.5, b["rr"][:, 0, :], ALU.mult, ALU.mult).then_inc(cs["kn"][g], 1)
                    dve.wait_ge(cs["kn"][g], c + 1)
                    dve.wait_ge(cs["eg"][g], c + 1)
                    dve.tensor_tensor(b["Qd"][:, :], b["KQ"][:, 1, :], b["EG"][:, :], ALU.mult).then_inc(cs["qd"][g], 1)
                for g in range(2):
                    b = B[g]
                    dve.wait_ge(cs["dec"][g], c * 2 + 2)
                    dve.wait_ge(cs["kk"][g], c + 1)
                    dve.wait_ge(cs["lt"][g], c * LEVELS)
                    dve.tensor_tensor(b["NT"][:, :], PS[0:C, 4 * g, 0:GW], b["dec"][0:C, :], ALU.mult).then_inc(cs["nt0"][g], 1)
                    dve.tensor_tensor(b["attn"][:, :], PS[0:C, 4 * g + 1, 0:GW], b["dec"][0:C, :], ALU.mult).then_inc(cs["att"][g], 1)
                    dve.wait_ge(cs["nt0"][g], c + 1)
                    dve.tensor_tensor(v3(b["NT"][:, :]), v3(b["NT"][:, :]),
                                      cur[:, 8 + HG * g:8 + HG * g + HG].unsqueeze(2).broadcast_to([C, HG, C]),
                                      ALU.mult).then_inc(cs["nt"][g], 1)
                idb = ident[0:C, 0:C].unsqueeze(1).broadcast_to([C, HG, C])
                for g in range(2):
                    b = B[g]
                    dve.wait_ge(cs["lt"][g], c * LEVELS + 1)
                    dve.tensor_tensor(v3(b["U"][:, :]), v3(b["LT"][:, 0, :]), idb, ALU.add).then_inc(cs["u1"][g], 1)
                for g in range(2):
                    b = B[g]
                    dve.wait_ge(cs["t1p"][g], c + 1)
                    dve.tensor_tensor(v3(b["T"][:, :]), v3(PS[0:C, 4 * g, 0:GW]), idb, ALU.add).then_inc(cs["t1"][g], 1)
                for v in range(LEVELS - 1):
                    for g in range(2):
                        b = B[g]
                        dve.wait_ge(cs["tu"][g], c * (LEVELS - 1) + v + 1)
                        dve.wait_ge(cs["t1"][g], c + 1)
                        if v < LEVELS - 2:
                            dve.tensor_tensor(b["T"][:, :], PS[0:C, 4 * g + 2, 0:GW], b["T"][:, :], ALU.add)
                        dve.tensor_tensor(b["U"][:, :], PS[0:C, 4 * g + 3, 0:GW], b["U"][:, :], ALU.add).then_inc(cs["u"][g], 1)
                        if v < LEVELS - 2:
                            dve.wait_ge(cs["u"][g], c * (LEVELS - 1) + v + 1)
                for g in range(2):
                    b = B[g]
                    dve.wait_ge(cs["up"][g], c + 1)
                    dve.tensor_tensor(b["u"][:, :].rearrange("p (h d) -> p h d", h=HG),
                                      PS[0:C, 4 * g + 1, :].rearrange("p (h d) -> p h d", h=HG),
                                      cur[:, 16 + HG * g:16 + HG * g + HG].unsqueeze(2).broadcast_to([C, HG, 128]),
                                      ALU.mult).then_inc(cs["us"][g], 1)
                for g in range(2):
                    b = B[g]
                    dve.wait_ge(cs["sm2"][g], c + 1)
                    dve.wait_ge(cs["sp"][g], c + 1)
                    dve.tensor_tensor(b["S"][:, :], PS[:, 4 * g + 3, :], b["S"][:, :], ALU.add).then_inc(cs["snew"][g], 1)
                dve.wait_ge(c_gate, c * 16 + 16)
                for g in range(2):
                    b = B[g]
                    dve.wait_ge(cs["orn"][g], c * 2 + 2)
                    dve.wait_ge(cs["oc"][g], c + 1)
                    dve.tensor_tensor(b["on"][:, :], b["o"][:, :], b["rr"][:, 0, :], ALU.mult).then_inc(cs["on1"][g], 1)
                    dve.wait_ge(cs["on1"][g], c + 1)
                    dve.scalar_tensor_tensor(b["on"][:, :], b["on"][:, :], pvec[:, ON:ON + 1],
                                             Gt[:, HG * g:HG * g + HG, :].rearrange("p h j -> p (h j)"),
                                             ALU.mult, ALU.mult).then_inc(cs["on2"][g], 1)
                for g in range(2):
                    b = B[g]
                    dve.wait_ge(cs["on2"][g], c + 1)
                    dve.wait_ge(cs["oh"][g], c + 1)
                    dst = slice(HG * g, HG * g + HG)
                    dve.tensor_tensor(XL[:, dst, ds(c * C, C)], v3(b["on"][:, :]),
                                      XH[:, dst, ds(c * C, C)].bitcast(F32), ALU.subtract).then_inc(cs["ol"][g], 1)

            def add_phase(ph):
                for s in range(4):
                    lo(s, ph.job0 + s + 1)
                for l in range(ph.jobs):
                    for ch, (t0, n) in enumerate(ph.chunks):
                        dve.wait_ge(mm_chunk, ph.mm0 + ph.nch * l + ch + 1)
                        dst = hT[:, l, t0:t0 + n]
                        dve.tensor_tensor(dst, PS[:, ph.nch * (l % 2) + ch, 0:n], dst, ALU.add).then_inc(taken, 1)
                    if l + 4 < ph.jobs:
                        lo(l % 4, ph.job0 + l + 5)

            def ffn(ph, layer):
                nch, chs = ph.nch, ph.chunks
                t00 = chs[0][0]
                W = chs[-1][0] + chs[-1][1] - t00
                DU = 8 * nch
                d0 = 0 if layer == 0 else 24 * FG
                a0 = 0 if layer == 0 else 6 * FG
                banks = down_banks(nch)
                lo(0, ph.job0 + 1)
                norm("f0" if layer == 0 else "f1")
                for s in range(1, 6):
                    lo(s, ph.job0 + s + 1)
                lo(0, ph.job0 + 7)

                def tile(g, t):
                    for ch, (t0, n) in enumerate(chs):
                        dve.wait_ge(silu_g, g * (2 * nch) + (a0 + nch * t + ch + 1))
                        dve.wait_ge(mm_chunk, g * (4 * nch) + (ph.mm0 + nch * (2 * t + 1) + ch + 1))
                        if ch == 0:
                            dve.wait_ge(act_h, g * 2 + (t + 2 * FG * layer))
                            dve.wait_ge(act_l, g * 2 + (t + 2 * FG * layer))
                        o = slice(t0 - t00, t0 - t00 + n)
                        dve.tensor_tensor(aact[:, o], PS[:, nch + ch, 0:n], gact[:, o], ALU.mult).then_inc(act_a, 1)
                    dve.wait_ge(act_h, g * 2 + (t + 1 + 2 * FG * layer))
                    dve.wait_ge(act_a, g * (2 * nch) + (a0 + nch * (t + 1)))
                    dve.tensor_tensor(AL[:, t, 0:W], aact[:, 0:W], AH[:, t, 0:W].bitcast(F32), ALU.subtract).then_inc(act_l, 1)

                def body(g, nxt):
                    j = ph.job0 + 7
                    tile(g, 0)
                    tile(g, 1)
                    if nxt:
                        for k, s in enumerate((1, 2, 3, 4)):
                            lo(s, g * 6 + (j + k + 1))
                    for u in range(DU):
                        ch, m = u // 8, u % 8
                        t0, n = chs[ch]
                        dve.wait_ge(d_mm, g * DU + (d0 + u + 1))
                        if u == 0:
                            dve.wait_ge(d_add, g * DU + d0)
                        dst = hT[:, m, t0:t0 + n]
                        dve.tensor_tensor(dst, PS[:, banks[u % len(banks)], 0:n], dst, ALU.add).then_inc(d_add, 1)
                    if nxt:
                        lo(5, g * 6 + (j + 5))
                    if nxt == 1:
                        lo(0, g * 6 + (j + 6))
                with dve.Fori(0, FG - 2) as g:
                    body(g, 1)
                body(FG - 2, 2)
                body(FG - 1, 0)

            for g in range(2):
                dve.wait_ge(cs["ol"][g], NC)
            add_phase(P_GO)
            ffn(P_F0, 0)
            for s in range(4):
                lo(s, P_KV.job0 + s + 1)
            norm("kv")
            for l in range(P_KV.jobs - 4):
                lo(l % 4, P_KV.job0 + l + 5)
            for s in range(4):
                lo(s, P_Q.job0 + s + 1)
            norm("sb")
            for l in range(P_Q.jobs - 4):
                lo(l % 4, P_Q.job0 + l + 5)

            dve.wait_ge(t_one, 2)
            dve.sem_inc(t_p, 1)
            dve.sem_inc(t_w, 1)

            def copy_groups(j, u):
                for n in group_numbers("W", u):
                    _, _, k0, nb, engine = GROUPS[n]
                    if engine != "dve":
                        continue
                    rows = META if k0 == 8 else 128
                    dve.wait_ge(t_tr, j * NGR + (n + 1))
                    free(dve, t_pv, j * 16 + max(u - 1, 0))
                    dve.tensor_copy(wT[u % 2][0:rows, k0:k0 + nb, :],
                                    PS[0:rows, 5 + n % 2, 0:128 * nb].rearrange("p (k n) -> p k n", n=128)).then_inc(t_cd, 1)

            with dve.Fori(0, PAIRS) as j:
                for u in range(2 * QB):
                    i, b = u % QB, u % 2
                    n = META + 128 * (i + 1)
                    dve.wait_ge(t_kp, j * 16 + (u + 1))
                    free(dve, t_w, j * 16 + u)
                    dve.tensor_tensor_scan(Pr[b][:, L - n:L][:, ::-1], kp[b][:, 0:n][:, ::-1], kp[b][:, 0:n][:, ::-1], 1.0,
                                           ALU.mult, ALU.bypass).then_inc(t_p, 1)
                    free(dve, t_p, j * 16 + (u + 1))
                    dve.wait_ge(t_sg, j * 16 + (u + 1))
                    dve.wait_ge(t_tr, j * NGR + (group_numbers("W", u - 2)[-1] + 1 if u >= 2 else 1))
                    dve.tensor_tensor(wt[b][:, 0:n], Pr[b][:, L - n + 1:L + 1], sg[b][:, 0:n], ALU.mult).then_inc(t_w, 1)
                    if u:
                        copy_groups(j, u - 1)
                copy_groups(j, 2 * QB - 1)

            add_phase(P_O)
            ffn(P_F1, 1)
            norm("fin")
            for t in range(QB):
                dve.wait_ge(o_tr, 2 * t + 2)
                if t >= 2:
                    dve.wait_ge(o_out[t % 2], 16 * (t // 2))
                dve.tensor_copy(fo[:, t % 2, 512:1024], PS[:, 5 + 2 * (t % 2), :]).then_inc(o_cpv, 1)

        @block.tensor
        def _(pe):
            def norm(name):
                chs, n0, _ = NORMS[name]
                for j, (t0, n) in enumerate(chs):
                    pe.wait_ge(sq_r, n0 + j + 1)
                    for k in range(KT):
                        m = pe.matmul(PS[:, j, 0:n], ones[:, :], sqb[:, k, 0:n], start=(k == 0), stop=(k == KT - 1))
                    m.then_inc(ss_r, 1)

            def chunk(s, bank, t0, n):
                for k in range(KT):
                    wh, wl = WH[s][:, 128 * k:128 * k + 128], WL[s][:, 128 * k:128 * k + 128]
                    xh, xl = XH[:, k, t0:t0 + n], XL[:, k, t0:t0 + n]
                    pe.matmul(PS[:, bank, 0:n], wl, xh, start=(k == 0), stop=False)
                    pe.matmul(PS[:, bank, 0:n], wh, xl, start=False, stop=False)
                    m = pe.matmul(PS[:, bank, 0:n], wh, xh, start=False, stop=(k == KT - 1))
                m.then_inc(mm_chunk, 1)

            pe.wait_ge(cst2, CONSTS)
            pe.wait_ge(x_in, 32)
            for t in range(9):
                n = META if t == 8 else 128
                if t >= 3:
                    pe.wait_ge(x_cpa, t - 2)
                    pe.wait_ge(x_cpv, t - 2)
                for half in range(2):
                    for k in range(4):
                        f = 4 * half + k
                        m = pe.transpose(PS[:, 2 * (t % 3) + half, 128 * k:128 * k + n], xin[0:n, t, 128 * f:128 * f + 128],
                                         ident[0:n, 0:n])
                    m.then_inc(x_tr, 1)
            pe.wait_ge(p_in, 16 * 7)
            pe.transpose(PS[:, 6, 0:121], prow[0:121, :], ident[0:121, 0:121]).then_inc(p_tr, 1)
            pe.transpose(PS[:, 7, 0:24], prow2[:, :], ident[0:24, 0:24]).then_inc(p_tr, 1)
            pe.wait_ge(x_cpa, 9)
            pe.wait_ge(x_cpv, 9)
            norm("gdn")
            pe.wait_ge(ab_l, 1)
            for ch, (t0, n) in enumerate(ALL_CH):
                pe.wait_ge(xl_r, ch + 1)
                for k in range(KT):
                    xh, xl = XH[:, k, t0:t0 + n], XL[:, k, t0:t0 + n]
                    o = PS[0:16, 3 + ch, 0:n]
                    pe.matmul(o, wabL[:, k, :], xh, start=(k == 0), stop=False)
                    pe.matmul(o, wabH[:, k, :], xl, start=False, stop=False)
                    m = pe.matmul(o, wabH[:, k, :], xh, start=False, stop=(k == KT - 1))
                m.then_inc(ab_mm, 1)
            pe.wait_ge(ab_cp, 3)
            pe.wait_ge(p_cp, 2)
            for c in range(NC):
                m = pe.transpose(PS[0:C, 6, 16 * c:16 * c + 16], cac[0:16, c * C:(c + 1) * C], ident[0:16, 0:16])
            m.then_inc(ab_mm, 1)

            with pe.Fori(0, GH) as h:
                for s in range(4):
                    pe.wait_ge(w_lo, h * 4 + s + 1)
                    for ch, (t0, n) in enumerate(ALL_CH):
                        if s >= 2:
                            pe.wait_ge(taken, h * 12 + (3 * s + ch - 5))
                        else:
                            pe.wait_ge(taken, h * 12)
                        chunk(s, 3 * (s % 2) + ch, t0, n)

            pe.wait_ge(sml, 12)
            pe.matmul(PS[0:C, 7, 0:8 * NC], tri[:, :], sm[:, :, 32:40], start=True, stop=True).then_inc(sml, 1)
            pe.wait_ge(sml, SMALL)
            pe.wait_ge(c_s0, 2)

            def hd(t, h, w=C):
                return t[:, h * w:(h + 1) * w]

            with pe.Fori(0, NC) as c:
                for g in range(2):
                    b, p0 = B[g], 4 * g
                    pe.wait_ge(cs["sq"][g], c + 1)
                    pe.wait_ge(cs["orn"][g], c * 2)
                    pe.wait_ge(cs["us"][g], c)
                    pe.matmul(PS[:, p0, 0:GW], ones[:, :], b["sq"][:, 0, :], start=True, stop=True)
                    pe.matmul(PS[:, p0 + 1, 0:GW], ones[:, :], b["sq"][:, 1, :], start=True, stop=True).then_inc(cs["ss"][g], 1)
                    pe.wait_ge(cs["tg"][g], c + 1)
                    pe.wait_ge(cs["oc"][g], c)
                    pe.matmul(PS[:, p0 + 2, 0:GW], ones[0:C, :], b["tg"][:, :], start=True, stop=True).then_inc(cs["gb"][g], 1)
                for g in range(2):
                    b, p0 = B[g], 4 * g
                    pe.wait_ge(cs["kn"][g], c + 1)
                    for h in range(HG):
                        pe.matmul(PS[0:C, p0, h * C:(h + 1) * C], hd(b["KQ"][:, 0, :], h), hd(b["KQ"][:, 0, :], h), start=True, stop=True)
                    for h in range(HG):
                        m = pe.matmul(PS[0:C, p0 + 1, h * C:(h + 1) * C], hd(b["KQ"][:, 0, :], h), hd(b["KQ"][:, 1, :], h), start=True, stop=True)
                    m.then_inc(cs["kk"][g], 1)
                    pe.wait_ge(cs["dm"][g], c + 1)
                    pe.wait_ge(cs["eg"][g], c + 1)
                    pe.wait_ge(cs["snew"][g], c)
                    for h in range(HG):
                        pe.transpose(PS[0:C, p0 + 2, h * 128:(h + 1) * 128], hd(b["KQ"][:, 0, :], h), ident[:, :])
                    for h in range(HG):
                        m = pe.transpose(PS[0:C, p0 + 3, h * 128:(h + 1) * 128], Xc[:, 16 + HG * g + h, :], ident[:, :])
                    m.then_inc(cs["tr"][g], 1)
                for g in range(2):
                    b, p0 = B[g], 4 * g
                    pe.wait_ge(cs["lt"][g], c * LEVELS + 1)
                    pe.wait_ge(cs["nt0"][g], c + 1)
                    for h in range(HG):
                        m = pe.transpose(PS[0:C, p0, h * C:(h + 1) * C], hd(b["LT"][:, 0, :], h), ident[0:C, 0:C])
                    m.then_inc(cs["t1p"][g], 1)
                for v in range(LEVELS - 1):
                    for g in range(2):
                        b, p0 = B[g], 4 * g
                        if v == 0:
                            pe.wait_ge(cs["t1"][g], c + 1)
                            pe.wait_ge(cs["u1"][g], c + 1)
                            pe.wait_ge(cs["att"][g], c + 1)
                            pe.wait_ge(cs["kt"][g], c + 1)
                        else:
                            pe.wait_ge(cs["u"][g], c * (LEVELS - 1) + v)
                        pe.wait_ge(cs["lt"][g], c * LEVELS + (v + 2))
                        pe.wait_ge(cs["xc"][g], c * (LEVELS - 1) + v)
                        for h in range(HG):
                            m = pe.matmul(PS[0:C, p0 + 1, h * C:(h + 1) * C], hd(b["LT"][:, (v + 1) % LTB, :], h), hd(b["T"], h), start=True, stop=True)
                        m.then_inc(cs["x"][g], 1)
                    for g in range(2):
                        b, p0 = B[g], 4 * g
                        pe.wait_ge(cs["xc"][g], c * (LEVELS - 1) + (v + 1))
                        for h in range(HG):
                            if v < LEVELS - 2:
                                pe.matmul(PS[0:C, p0 + 2, h * C:(h + 1) * C], hd(b["U"], h), hd(b["X"], h), start=True, stop=True)
                        for h in range(HG):
                            m = pe.matmul(PS[0:C, p0 + 3, h * C:(h + 1) * C], hd(b["X"], h), hd(b["U"], h), start=True, stop=True)
                        m.then_inc(cs["tu"][g], 1)
                for g in range(2):
                    b, p0 = B[g], 4 * g
                    pe.wait_ge(cs["u"][g], c * (LEVELS - 1) + (LEVELS - 1))
                    pe.wait_ge(cs["kde"][g], c * 2 + 2)
                    for h in range(HG):
                        m = pe.matmul(PS[:, p0, h * C:(h + 1) * C], hd(b["Ke"], h, 128), hd(b["U"], h), start=True, stop=True)
                    m.then_inc(cs["wt"][g], 1)
                for g in range(2):
                    b, p0 = B[g], 4 * g
                    pe.wait_ge(cs["wtc"][g], c + 1)
                    pe.wait_ge(cs["snew"][g], c)
                    for h in range(HG):
                        o = PS[0:C, p0 + 1, h * 128:(h + 1) * 128]
                        pe.matmul(o, hd(b["U"], h), hd(b["V"], h, 128), start=True, stop=False)
                        m = pe.matmul(o, hd(b["WT"], h), hd(b["S"], h, 128), start=False, stop=True)
                    m.then_inc(cs["up"][g], 1)
                for g in range(2):
                    b, p0 = B[g], 4 * g
                    pe.wait_ge(cs["us"][g], c + 1)
                    pe.wait_ge(cs["qd"][g], c + 1)
                    for h in range(HG):
                        o = PS[:, p0 + 2, h * C:(h + 1) * C]
                        pe.matmul(o, hd(b["S"], h, 128), hd(b["Qd"], h), start=True, stop=False)
                        m = pe.matmul(o, hd(b["u"], h, 128), hd(b["attn"], h), start=False, stop=True)
                    m.then_inc(cs["op"][g], 1)
                    for h in range(HG):
                        m = pe.matmul(PS[:, p0 + 3, h * 128:(h + 1) * 128], hd(b["Kd"], h, 128), hd(b["u"], h, 128), start=True, stop=True)
                    m.then_inc(cs["sp"][g], 1)
                for g in range(2):
                    b, p0 = B[g], 4 * g
                    pe.wait_ge(cs["osq"][g], c + 1)
                    pe.matmul(PS[:, p0, 0:GW], ones[:, :], b["sq"][:, 0, :], start=True, stop=True).then_inc(cs["oss"][g], 1)
            for g in range(2):
                pe.wait_ge(cs["ol"][g], NC)

            def dense(ph, norm_name):
                t_base = TAKEN0[ph]
                for l in range(ph.jobs):
                    s = l % 4
                    pe.wait_ge(w_lo, ph.job0 + l + 1)
                    for ch, (t0, n) in enumerate(ph.chunks):
                        if l == 0 and norm_name:
                            pe.wait_ge(xl_r, xn_needed(norm_name, ph, ch))
                        if l >= 2:
                            pe.wait_ge(taken, t_base + ph.nch * (l - 2) + ch + 1)
                        chunk(s, ph.nch * (l % 2) + ch, t0, n)

            def ffn(ph, layer, name):
                nch, chs = ph.nch, ph.chunks
                DU = 8 * nch
                d0 = 0 if layer == 0 else 24 * FG
                s0 = 0 if layer == 0 else 6 * FG
                banks = down_banks(nch)
                t00 = chs[0][0]
                pe.wait_ge(w_lo, ph.job0 + 1)
                for ch, (t0, n) in enumerate(chs):
                    pe.wait_ge(xl_r, xn_needed(name, ph, ch))
                    chunk(0, ch, t0, n)

                def down(g, sa, sb):
                    pe.wait_ge(act_l, g * 2 + (2 + 2 * FG * layer))
                    for u in range(DU):
                        ch, m = u // 8, u % 8
                        t0, n = chs[ch]
                        bank = PS[:, banks[u % len(banks)], 0:n]
                        if u >= len(banks):
                            pe.wait_ge(d_add, g * DU + (d0 + u - len(banks) + 1))
                        for t, s in ((0, sa), (1, sb)):
                            wh, wl = WH[s][:, 128 * m:128 * m + 128], WL[s][:, 128 * m:128 * m + 128]
                            ah, al = AH[:, t, t0 - t00:t0 - t00 + n], AL[:, t, t0 - t00:t0 - t00 + n]
                            pe.matmul(bank, wl, ah, start=(t == 0), stop=False)
                            pe.matmul(bank, wh, al, start=False, stop=False)
                            y = pe.matmul(bank, wh, ah, start=False, stop=(t == 1))
                        y.then_inc(d_mm, 1)

                def body(g, last):
                    j = ph.job0 + 1
                    for k, (s, bank0) in enumerate(((1, nch), (2, 0), (3, nch), (4, 0))):
                        if k == 3 and last:
                            break
                        pe.wait_ge(w_lo, g * 6 + (j + k + 1))
                        if k == 0:
                            pe.wait_ge(d_add, g * DU + d0)
                        if k == 1:
                            pe.wait_ge(silu_g, g * (2 * nch) + (s0 + nch))
                        if k == 2:
                            pe.wait_ge(act_a, g * (2 * nch) + (s0 + nch))
                        if k == 3:
                            pe.wait_ge(silu_g, g * (2 * nch) + (s0 + 2 * nch))
                        for ch, (t0, n) in enumerate(chs):
                            chunk(s, bank0 + ch, t0, n)
                    if last:
                        pe.wait_ge(w_lo, g * 6 + (j + 5))
                        down(g, 4, 5)
                    else:
                        pe.wait_ge(w_lo, g * 6 + (j + 6))
                        down(g, 5, 0)
                with pe.Fori(0, FG - 1) as g:
                    body(g, False)
                body(FG - 1, True)

            dense(P_GO, None)
            norm("f0")
            ffn(P_F0, 0, "f0")
            norm("kv")
            dense(P_KV, "kv")
            norm("sb")
            dense(P_Q, "sb")

            PSf = PS[:, :, :].rearrange("p b n -> p (b n)")
            pe.wait_ge(taken, TAKEN0[P_O])

            def scores(j, u):
                h, i, b = u // QB % 2, u % QB, u % 2
                n, q = META + 128 * (i + 1), QS[h][:, 128 * i:128 * i + 128]
                if i == 0:
                    pe.wait_ge(t_lo, j * 4 + (2 * (u // QB) + 2))
                if u >= 2:
                    pe.wait_ge(t_sg, j * 16 + (u - 1))
                for c0 in range(0, n, 512):
                    c1 = min(c0 + 512, n)
                    m0 = max(c0, n - 128)
                    z = PSf[:, Z0[b] + c0:Z0[b] + c1]
                    pe.matmul(z, q, KL[h][:, c0:c1], start=True, stop=False)
                    m = pe.matmul(z, q, KH[h][:, c0:c1], start=False, stop=m0 >= c1)
                    if m0 < c1:
                        m = pe.matmul(PSf[:, Z0[b] + m0:Z0[b] + c1], identb[:, :], maskb[:, m0 - n + 128:c1 - n + 128],
                                      start=False, stop=True)
                m.then_inc(t_z, 1)

            def group(j, n):
                kind, u, k0, nb, _ = GROUPS[n]
                if n < 2:
                    free(pe, t_ca, j * copied(NGR, "act"))
                elif GROUPS[n - 2][4] == "act":
                    free(pe, t_ca, j * copied(NGR, "act") + copied(n - 1, "act"))
                else:
                    pe.wait_ge(t_cd, j * copied(NGR, "dve") + copied(n - 1, "dve"))
                for k in range(k0, k0 + nb):
                    r0, rn = (0, META) if k == 8 else (META + 128 * k, 128)
                    src = {"V": vT[:, r0:r0 + rn], "W": wt[u % 2][:, r0:r0 + rn], "O": ot[:, min(k, 7), :]}[kind]
                    if kind == "O":
                        rn = 128
                    m = pe.transpose(PS[0:rn, 5 + n % 2, 128 * (k - k0):128 * (k - k0) + 128], src, ident[:, :])
                m.then_inc(t_tr, 1)

            def weigh(j, u):
                i, h = u % QB, u // QB
                gs = group_numbers("W", u)
                for n in gs:
                    _, _, k0, nb, engine = GROUPS[n]
                    if engine == "act":
                        free(pe, t_ca, j * copied(NGR, "act") + copied(n + 1, "act"))
                    else:
                        pe.wait_ge(t_cd, j * copied(NGR, "dve") + copied(n + 1, "dve"))
                    if u == QB and n == gs[0]:
                        pe.wait_ge(t_o, j * 2 + 1)
                    for k in range(k0, k0 + nb):
                        rn = META if k == 8 else 128
                        m = pe.matmul(PS[:, 7, 64 * i:64 * i + 64], wT[u % 2][0:rn, k, :], Vt[0:rn, k, 64 * h:64 * h + 64],
                                      start=(k == 0), stop=(n == gs[-1]))
                m.then_inc(t_pv, 1)

            def pair(j, last):
                pe.wait_ge(t_vload, j * 16 + 16)
                for n in group_numbers("V"):
                    group(j, n)
                for u in range(2 * QB):
                    pe.wait_ge(t_w, j * 16 + (u + 2))
                    ns = group_numbers("W", u)
                    group(j, ns[0])
                    if not (last and u + 2 >= 2 * QB):
                        scores(j, u + 2)
                    for n in ns[1:]:
                        group(j, n)
                    if u:
                        weigh(j, u - 1)
                weigh(j, 2 * QB - 1)
                pe.wait_ge(t_o, j * 2 + 2)
                for n in group_numbers("O"):
                    group(j, n)

            pe.sem_inc(t_pv, 1)
            scores(0, 0)
            scores(0, 1)
            with pe.Fori(0, PAIRS - 1) as j:
                pair(j, False)
            pair(PAIRS - 1, True)
            free(pe, t_ol, PAIRS)
            dense(P_O, None)
            norm("f1")
            ffn(P_F1, 1, "f1")
            norm("fin")
            for t in range(QB):
                if t == 0:
                    pe.wait_ge(d_add, 24 * FG + 16 * FG)
                pe.wait_ge(xn_r, XL0["fin"] + t // 2 + 1)
                if t >= 2:
                    pe.wait_ge(o_cpa, t - 1)
                    pe.wait_ge(o_cpv, t - 1)
                for half in range(2):
                    for k in range(4):
                        m = pe.transpose(PS[:, 4 + 2 * (t % 2) + half, 128 * k:128 * k + 128],
                                         hT[:, 4 * half + k, META + 128 * t:META + 128 * t + 128], ident[:, :])
                    m.then_inc(o_tr, 1)


_INS = ["x", "meta_tokens", "gdn_norm_g", "gdn_w_in", "gdn_conv_w", "gdn_a_log", "gdn_dt_bias", "gdn_onorm_g",
        "gdn_w_out", "kv_norm_g", "w_kv", "sb_norm_g", "sb_w_q", "sb_w_o", "ffn_norm_g", "ffn_w_gate_up",
        "ffn_w_down", "final_norm_g"]


def kernel(**inputs):
    import numpy as _np
    import concourse.bacc as _bacc
    from concourse import mybir as _mybir
    from concourse.bass_utils import run_bass_kernel_spmd as _run

    nc = _bacc.Bacc("TRN2", target_bir_lowering=False, num_devices=1)
    arrays, args = {}, []
    for name in _INS:
        a = _np.ascontiguousarray(inputs[name])
        arrays[f"in_{name}"] = a
        args.append(nc.dram_tensor(f"in_{name}", a.shape, _mybir.dt.from_np(a.dtype), kind="ExternalInput").ap())
    out = nc.dram_tensor("out_0", (1, SEQ, D), _mybir.dt.float32, kind="ExternalOutput").ap()
    trunk(nc, *args, out)
    r = _run(nc, [arrays], core_ids=[0])
    return r.results[0]["out_0"]
```
